# Optimizing a Trainium2 kernel written in Bass

```python
import jax, jax.numpy as jnp
from jax import lax
import numpy as np
import math

D_MODEL = 2048
BATCH = 1
SEQ = 512
DEPTH = 1

CHUNK = 64
D_MIX = D_MODEL
D_CONV = D_MIX // 2
CONV_GROUPS = 16
D_RWKV = D_MIX - D_CONV
RWKV_HEAD = 64
N_RWKV_HEADS = D_RWKV // RWKV_HEAD
CONV_WIDTH = 31
D_DECAY_LORA = 64
D_AAA_LORA = 64
D_GATE_LORA = 160
N_GROUPS = 4
EXPERTS_PER_GROUP = 8
N_EXPERTS = N_GROUPS * EXPERTS_PER_GROUP
TOP_K = 2
D_EXPERT = 512
MOE_BLOCK = 128
RMS_EPS = 1e-6
LN_EPS = 1e-5
GN_EPS = 64e-5
D_IN = 2 * D_CONV + 3 * D_RWKV + D_DECAY_LORA + D_AAA_LORA + D_GATE_LORA
D_SHIFT = D_IN - 2 * D_CONV


def rms_norm(x, g):
    xf = x.astype(jnp.float32)
    y = xf * lax.rsqrt(jnp.mean(xf * xf, axis=-1, keepdims=True) + RMS_EPS)
    return (y * g.astype(jnp.float32)).astype(x.dtype)

def layer_norm(u, g, b):
    uf = u.astype(jnp.float32)
    mu = jnp.mean(uf, axis=-1, keepdims=True)
    var = jnp.mean(jnp.square(uf - mu), axis=-1, keepdims=True)
    y = (uf - mu) * lax.rsqrt(var + LN_EPS) * g.astype(jnp.float32) + b.astype(jnp.float32)
    return y.astype(u.dtype)

def prev_frame(u):
    return jnp.pad(u, ((0, 0), (1, 0), (0, 0)))[:, :-1]

def conformer_conv(val, gate, dw, bias, ln_g, ln_b):
    u = val * jax.nn.sigmoid(gate)
    u = lax.conv_general_dilated(
        u, dw[:, None, :].astype(u.dtype), window_strides=(1,),
        padding=[(CONV_WIDTH - 1, 0)], dimension_numbers=('NWC', 'WIO', 'NWC'),
        feature_group_count=D_CONV) + bias
    u = layer_norm(u, ln_g, ln_b)
    return jax.nn.silu(u)

def rwkv7_scan(r, decay, k, v, a, b):
    B, T, H, N = r.shape
    def step(S, inp):
        rt, wt, kt, vt, at, bt = inp
        sa = jnp.einsum('bhvk,bhk->bhv', S, at)
        S = S * wt[:, :, None, :] + sa[..., None] * bt[:, :, None, :] + vt[..., None] * kt[:, :, None, :]
        return S, jnp.einsum('bhvk,bhk->bhv', S, rt)
    S0 = jnp.zeros((B, H, N, N), jnp.float32)
    xs = tuple(jnp.moveaxis(t, 1, 0) for t in (r, decay, k, v, a, b))
    _, y = lax.scan(step, S0, xs)
    return jnp.moveaxis(y, 0, 1)

def rwkv7_time_mix(proj, mu, w0, w_up, a0, a_up, g_up, k_k, k_a, r_k, gn_g, gn_b):
    B, T, _ = proj.shape
    f32 = jnp.float32
    proj = proj + (prev_frame(proj) - proj) * mu
    o1, o2, o3 = D_RWKV, 2 * D_RWKV, 3 * D_RWKV
    r, k, v, wd, ad, gd = jnp.split(
        proj, [o1, o2, o3, o3 + D_DECAY_LORA, o3 + D_DECAY_LORA + D_AAA_LORA], axis=-1)
    w = -jax.nn.softplus(-(w0 + jnp.tanh(wd) @ w_up)) - 0.5
    decay = jnp.exp(-jnp.exp(w.astype(f32)))
    a = jax.nn.sigmoid(a0 + ad @ a_up).astype(f32)
    g = jax.nn.sigmoid(gd) @ g_up
    heads = lambda t: t.astype(f32).reshape(B, T, N_RWKV_HEADS, RWKV_HEAD)
    kk = heads(k * k_k)
    kk = kk / jnp.maximum(jnp.sqrt(jnp.sum(kk * kk, axis=-1, keepdims=True)), 1e-12)
    k = k.astype(f32) * (1.0 + (a - 1.0) * k_a.astype(f32))
    rh, kh, vh, ah, wh = heads(r), heads(k), heads(v), heads(a), heads(decay)
    y = rwkv7_scan(rh, wh, kh, vh, -kk, kk * ah)
    mu_y = jnp.mean(y, axis=-1, keepdims=True)
    var_y = jnp.mean(jnp.square(y - mu_y), axis=-1, keepdims=True)
    y = ((y - mu_y) * lax.rsqrt(var_y + GN_EPS)).reshape(B, T, D_RWKV)
    y = y * gn_g.astype(f32) + gn_b.astype(f32)
    bonus = jnp.sum(rh * kh * r_k.astype(f32), axis=-1, keepdims=True) * vh
    y = y + bonus.reshape(B, T, D_RWKV)
    return (y * g.astype(f32)).astype(proj.dtype)

def hierarchical_moe(h, rg_w, rg_b, re_w, re_b, w_gate, w_up, w_down):
    B, T, D = h.shape
    xt = h.reshape(-1, D)
    NT = xt.shape[0]
    xf = xt.astype(jnp.float32)
    g_logits = xf @ rg_w.astype(jnp.float32) + rg_b.astype(jnp.float32)
    g_prob = jax.nn.softmax(g_logits, axis=-1)
    grp = jnp.argmax(g_logits, axis=-1)
    p_grp = jnp.take_along_axis(g_prob, grp[:, None], axis=-1)
    e_logits = (xf @ re_w.astype(jnp.float32) + re_b.astype(jnp.float32))
    e_logits = e_logits.reshape(NT, N_GROUPS, EXPERTS_PER_GROUP)
    e_logits = jnp.take_along_axis(e_logits, grp[:, None, None], axis=1)[:, 0]
    top_v, top_i = lax.top_k(e_logits, TOP_K)
    gates = p_grp * jax.nn.softmax(top_v, axis=-1)
    expert_id = (grp[:, None] * EXPERTS_PER_GROUP + top_i).astype(jnp.int32)

    A = NT * TOP_K
    flat_e = expert_id.reshape(-1)
    flat_tok = jnp.repeat(jnp.arange(NT, dtype=jnp.int32), TOP_K)
    flat_gate = gates.reshape(-1)
    order = jnp.argsort(flat_e)
    se, stok, sgate = flat_e[order], flat_tok[order], flat_gate[order]
    counts = jnp.zeros((N_EXPERTS,), jnp.int32).at[flat_e].add(1)
    starts = jnp.cumsum(counts) - counts
    padded = (counts + MOE_BLOCK - 1) // MOE_BLOCK * MOE_BLOCK
    pend = jnp.cumsum(padded)
    pstarts = pend - padded
    dest = pstarts[se] + (jnp.arange(A, dtype=jnp.int32) - starts[se])
    n_blocks = (A + N_EXPERTS * (MOE_BLOCK - 1) + MOE_BLOCK - 1) // MOE_BLOCK
    P = n_blocks * MOE_BLOCK
    slot_tok = jnp.full((P,), NT, jnp.int32).at[dest].set(stok)
    slot_gate = jnp.zeros((P,), jnp.float32).at[dest].set(sgate)
    block_e = jnp.minimum(
        jnp.searchsorted(pend, jnp.arange(n_blocks, dtype=jnp.int32) * MOE_BLOCK, side='right'),
        N_EXPERTS - 1)
    x_pad = jnp.concatenate([xt, jnp.zeros((1, D), xt.dtype)], axis=0)
    xb = x_pad[slot_tok].reshape(n_blocks, MOE_BLOCK, D)

    def expert_block(args):
        xblk, e = args
        hid = jax.nn.silu(xblk @ w_gate[e]) * (xblk @ w_up[e])
        return hid @ w_down[e]

    yb = lax.map(expert_block, (xb, block_e))
    y = yb.reshape(P, D) * slot_gate[:, None].astype(yb.dtype)
    out = jnp.zeros((NT + 1, D), yb.dtype).at[slot_tok].add(y)[:NT]
    return out.reshape(B, T, D).astype(h.dtype)

def first_inputs(seed: int = 0) -> dict:
    key = jax.random.key(seed)
    ks = jax.random.split(key, 28)
    f32 = jnp.float32
    L = DEPTH
    def nrm(k, shape, scale):
        return jax.random.normal(k, shape, f32) * scale
    return {
        'x': nrm(ks[0], (BATCH, SEQ, D_MODEL), 1.0),
        'norm_mix': 1.0 + nrm(ks[1], (L, D_MODEL), 0.02),
        'w_in': nrm(ks[2], (L, D_MODEL, D_IN), D_MODEL ** -0.5),
        'conv_dw': nrm(ks[3], (L, CONV_WIDTH, D_CONV), CONV_WIDTH ** -0.5),
        'conv_b': nrm(ks[4], (L, D_CONV), 0.02),
        'conv_ln_g': 1.0 + nrm(ks[5], (L, D_CONV), 0.02),
        'conv_ln_b': nrm(ks[6], (L, D_CONV), 0.02),
        'shift_mu': jax.random.uniform(ks[7], (L, D_SHIFT), f32),
        'w0': -1.0 + nrm(ks[8], (L, D_RWKV), 0.5),
        'w_lora_up': nrm(ks[9], (L, D_DECAY_LORA, D_RWKV), 0.1 * D_DECAY_LORA ** -0.5),
        'a0': nrm(ks[10], (L, D_RWKV), 0.5),
        'a_lora_up': nrm(ks[11], (L, D_AAA_LORA, D_RWKV), 0.1 * D_AAA_LORA ** -0.5),
        'g_lora_up': nrm(ks[12], (L, D_GATE_LORA, D_RWKV), D_GATE_LORA ** -0.5),
        'k_k': 0.85 + nrm(ks[13], (L, D_RWKV), 0.05),
        'k_a': 1.0 + nrm(ks[14], (L, D_RWKV), 0.05),
        'r_k': nrm(ks[15], (L, N_RWKV_HEADS, RWKV_HEAD), 0.1),
        'gn_g': 1.0 + nrm(ks[16], (L, D_RWKV), 0.02),
        'gn_b': nrm(ks[17], (L, D_RWKV), 0.02),
        'w_out': nrm(ks[18], (L, D_MIX, D_MODEL), D_MIX ** -0.5),
        'norm_ffn': 1.0 + nrm(ks[19], (L, D_MODEL), 0.02),
        'router_group_w': nrm(ks[20], (L, D_MODEL, N_GROUPS), D_MODEL ** -0.5),
        'router_group_b': nrm(ks[21], (L, N_GROUPS), 0.01),
        'router_expert_w': nrm(ks[22], (L, D_MODEL, N_EXPERTS), D_MODEL ** -0.5),
        'router_expert_b': nrm(ks[23], (L, N_EXPERTS), 0.01),
        'expert_w_gate': nrm(ks[24], (L, N_EXPERTS, D_MODEL, D_EXPERT), D_MODEL ** -0.5),
        'expert_w_up': nrm(ks[25], (L, N_EXPERTS, D_MODEL, D_EXPERT), D_MODEL ** -0.5),
        'expert_w_down': nrm(ks[26], (L, N_EXPERTS, D_EXPERT, D_MODEL), D_EXPERT ** -0.5),
        'norm_final': 1.0 + nrm(ks[27], (D_MODEL,), 0.02),
    }

def first_block(x, norm_mix, w_in, conv_dw, conv_b, conv_ln_g, conv_ln_b, shift_mu, w0,
              w_lora_up, a0, a_lora_up, g_lora_up, k_k, k_a, r_k, gn_g, gn_b, w_out,
              norm_ffn, router_group_w, router_group_b, router_expert_w, router_expert_b,
              expert_w_gate, expert_w_up, expert_w_down, norm_final):
    h = x
    for l in range(DEPTH):
        u = rms_norm(h, norm_mix[l])
        proj = u @ w_in[l]
        conv_val = proj[..., :D_CONV]
        conv_gate = proj[..., D_CONV:2 * D_CONV]
        rwkv_cols = proj[..., 2 * D_CONV:]
        y_conv = conformer_conv(conv_val, conv_gate, conv_dw[l], conv_b[l], conv_ln_g[l], conv_ln_b[l])
        y_rwkv = rwkv7_time_mix(rwkv_cols, shift_mu[l], w0[l], w_lora_up[l], a0[l], a_lora_up[l],
                                g_lora_up[l], k_k[l], k_a[l], r_k[l], gn_g[l], gn_b[l])
        mixed = jnp.concatenate([y_conv, y_rwkv], axis=-1)
        h = h + mixed @ w_out[l]
        v = rms_norm(h, norm_ffn[l])
        h = h + hierarchical_moe(v, router_group_w[l], router_group_b[l], router_expert_w[l],
                                 router_expert_b[l], expert_w_gate[l], expert_w_up[l], expert_w_down[l])
    return rms_norm(h, norm_final)


HEAD_DIM = 64
N_Q_HEADS = D_MODEL // 128
N_KV_HEADS = 4
Q_PER_KV = N_Q_HEADS // N_KV_HEADS
ATTN_W = N_Q_HEADS * HEAD_DIM
KV_W = N_KV_HEADS * HEAD_DIM
WINDOW = 128
BLOCK = 128
SSM_W = D_MODEL // 2
GROUP = 16
N_GROUPS_2 = SSM_W // GROUP
STATE = 64
IN_SIZES = (ATTN_W, KV_W, KV_W, ATTN_W, SSM_W, SSM_W, D_MODEL, D_MODEL)
IN_W = sum(IN_SIZES)
NORM_EPS = 1e-6


def rms_norm_2(x, w):
    xf = x.astype(jnp.float32)
    y = xf * lax.rsqrt(jnp.mean(xf * xf, axis=-1, keepdims=True) + NORM_EPS)
    return (y * w.astype(jnp.float32)).astype(x.dtype)

def sliding_window_attention(q, k, v, sinks):
    b, l = q.shape[0], q.shape[1]
    nb = l // BLOCK
    qb = q.reshape(b, nb, BLOCK, N_KV_HEADS, Q_PER_KV, HEAD_DIM)
    kb = k.reshape(b, nb, BLOCK, N_KV_HEADS, HEAD_DIM)
    vb = v.reshape(b, nb, BLOCK, N_KV_HEADS, HEAD_DIM)
    k_prev = jnp.concatenate([jnp.zeros_like(kb[:, :1]), kb[:, :-1]], axis=1)
    v_prev = jnp.concatenate([jnp.zeros_like(vb[:, :1]), vb[:, :-1]], axis=1)
    kk = jnp.concatenate([k_prev, kb], axis=2)
    vv = jnp.concatenate([v_prev, vb], axis=2)
    scale = 1.0 / math.sqrt(HEAD_DIM)
    scores = jnp.einsum('bnqgrd,bnsgd->bngrqs', qb, kk).astype(jnp.float32) * scale
    q_loc = jnp.arange(BLOCK)[:, None] + BLOCK
    k_loc = jnp.arange(2 * BLOCK)[None, :]
    diff = q_loc - k_loc
    k_abs = (jnp.arange(nb)[:, None, None] - 1) * BLOCK + k_loc[None]
    valid = (diff >= 0)[None] & (diff < WINDOW)[None] & (k_abs >= 0)
    scores = jnp.where(valid[None, :, None, None], scores, -1e30)
    sink = jnp.broadcast_to(
        sinks.astype(jnp.float32).reshape(1, 1, N_KV_HEADS, Q_PER_KV, 1, 1),
        scores.shape[:-1] + (1,))
    probs = jax.nn.softmax(jnp.concatenate([scores, sink], axis=-1), axis=-1)[..., :-1]
    out = jnp.einsum('bngrqs,bnsgd->bnqgrd', probs.astype(v.dtype), vv)
    return out.reshape(b, l, ATTN_W)

def s5_ssm(u, A_re, A_im, log_dt, B_re, B_im, C_re, C_im, D_skip):
    dt = jnp.exp(log_dt)[:, None]
    mag = jnp.exp(dt * A_re)
    ab_re = mag * jnp.cos(dt * A_im)
    ab_im = mag * jnp.sin(dt * A_im)
    num_re = ab_re - 1.0
    num_im = ab_im
    den = A_re * A_re + A_im * A_im
    cf_re = (num_re * A_re + num_im * A_im) / den
    cf_im = (num_im * A_re - num_re * A_im) / den
    bu_re = jnp.einsum('blgh,gph->blgp', u, B_re)
    bu_im = jnp.einsum('blgh,gph->blgp', u, B_im)
    b_re = cf_re * bu_re - cf_im * bu_im
    b_im = cf_re * bu_im + cf_im * bu_re
    a_re = jnp.broadcast_to(ab_re, b_re.shape)
    a_im = jnp.broadcast_to(ab_im, b_im.shape)

    def combine(e1, e2):
        a1r, a1i, b1r, b1i = e1
        a2r, a2i, b2r, b2i = e2
        return (a2r * a1r - a2i * a1i,
                a2r * a1i + a2i * a1r,
                a2r * b1r - a2i * b1i + b2r,
                a2r * b1i + a2i * b1r + b2i)

    _, _, s_re, s_im = lax.associative_scan(combine, (a_re, a_im, b_re, b_im), axis=1)
    y = (jnp.einsum('blgp,ghp->blgh', s_re, C_re)
         - jnp.einsum('blgp,ghp->blgh', s_im, C_im)
         + D_skip * u)
    return y

def second_inputs(seed: int = 0) -> dict:
    key = jax.random.key(seed)
    ks = jax.random.split(key, 20)
    f32 = jnp.float32
    n = jnp.arange(STATE, dtype=f32)
    x = jax.random.normal(ks[0], (BATCH, SEQ, D_MODEL), f32)
    norm_w = 1.0 + 0.02 * jax.random.normal(ks[1], (D_MODEL,), f32)
    w_in = jax.random.normal(ks[2], (D_MODEL, IN_W), f32) * D_MODEL ** -0.5
    q_norm_w = 1.0 + 0.02 * jax.random.normal(ks[3], (HEAD_DIM,), f32)
    k_norm_w = 1.0 + 0.02 * jax.random.normal(ks[4], (HEAD_DIM,), f32)
    sinks = jax.random.normal(ks[5], (N_Q_HEADS,), f32)
    w_attn_proj = jax.random.normal(ks[6], (ATTN_W, D_MODEL), f32) * ATTN_W ** -0.5
    A_re = -0.5 + 0.01 * jax.random.normal(ks[7], (N_GROUPS_2, STATE), f32)
    A_im = math.pi * n[None, :] + 0.01 * jax.random.normal(ks[8], (N_GROUPS_2, STATE), f32)
    log_dt = jax.random.uniform(ks[9], (N_GROUPS_2,), f32, math.log(1e-3), math.log(1e-1))
    b_scale = (2.0 * GROUP) ** -0.5
    B_re = jax.random.normal(ks[10], (N_GROUPS_2, STATE, GROUP), f32) * b_scale
    B_im = jax.random.normal(ks[11], (N_GROUPS_2, STATE, GROUP), f32) * b_scale
    c_scale = (2.0 * STATE) ** -0.5
    C_re = jax.random.normal(ks[12], (N_GROUPS_2, GROUP, STATE), f32) * c_scale
    C_im = jax.random.normal(ks[13], (N_GROUPS_2, GROUP, STATE), f32) * c_scale
    D_skip = jax.random.normal(ks[14], (N_GROUPS_2, GROUP), f32)
    w_glu = jax.random.normal(ks[15], (SSM_W, 2 * SSM_W), f32) * SSM_W ** -0.5
    b_glu = 0.01 * jax.random.normal(ks[16], (2 * SSM_W,), f32)
    w_ssm_proj = jax.random.normal(ks[17], (SSM_W, D_MODEL), f32) * SSM_W ** -0.5
    w_out = jax.random.normal(ks[18], (D_MODEL, D_MODEL), f32) * D_MODEL ** -0.5
    return {"x": x, "norm_w": norm_w, "w_in": w_in, "q_norm_w": q_norm_w,
            "k_norm_w": k_norm_w, "sinks": sinks, "w_attn_proj": w_attn_proj,
            "A_re": A_re, "A_im": A_im, "log_dt": log_dt, "B_re": B_re, "B_im": B_im,
            "C_re": C_re, "C_im": C_im, "D_skip": D_skip, "w_glu": w_glu,
            "b_glu": b_glu, "w_ssm_proj": w_ssm_proj, "w_out": w_out}

def second_block(x, norm_w, w_in, q_norm_w, k_norm_w, sinks, w_attn_proj, A_re, A_im,
              log_dt, B_re, B_im, C_re, C_im, D_skip, w_glu, b_glu, w_ssm_proj, w_out):
    b, l, _ = x.shape
    split_pts = list(np.cumsum(IN_SIZES)[:-1])
    f32 = jnp.float32
    for _layer in range(DEPTH):
        h = rms_norm_2(x, norm_w)
        proj = h @ w_in
        q, k, v, a_gate, u, z, g_a, g_s = jnp.split(proj, split_pts, axis=-1)
        q = rms_norm_2(q.reshape(b, l, N_Q_HEADS, HEAD_DIM), q_norm_w)
        k = rms_norm_2(k.reshape(b, l, N_KV_HEADS, HEAD_DIM), k_norm_w)
        v = v.reshape(b, l, N_KV_HEADS, HEAD_DIM)
        attn = sliding_window_attention(q, k, v, sinks)
        y_a = (attn * jax.nn.silu(a_gate)) @ w_attn_proj
        u_g = u.reshape(b, l, N_GROUPS_2, GROUP).astype(f32)
        y_ssm = s5_ssm(u_g, A_re.astype(f32), A_im.astype(f32), log_dt.astype(f32),
                       B_re.astype(f32), B_im.astype(f32), C_re.astype(f32),
                       C_im.astype(f32), D_skip.astype(f32))
        y_ssm = jax.nn.gelu(y_ssm.reshape(b, l, SSM_W)).astype(x.dtype)
        glu_a, glu_b = jnp.split(y_ssm @ w_glu + b_glu, 2, axis=-1)
        y_s = (glu_a * jax.nn.sigmoid(glu_b) * jax.nn.silu(z)) @ w_ssm_proj
        merged = jax.nn.sigmoid(g_a) * y_a + jax.nn.sigmoid(g_s) * y_s
        x = x + merged @ w_out
    return x


def setup_inputs(seed=0):
    out = dict(first_inputs(seed))
    for name, value in second_inputs(seed + 1).items():
        if name != "x":
            out[name + "_2"] = value
    return out


def reference(
    x, norm_mix, w_in, conv_dw, conv_b, conv_ln_g, conv_ln_b, shift_mu, w0, w_lora_up, a0,
    a_lora_up, g_lora_up, k_k, k_a, r_k, gn_g, gn_b, w_out, norm_ffn, router_group_w,
    router_group_b, router_expert_w, router_expert_b, expert_w_gate, expert_w_up, expert_w_down,
    norm_final, norm_w_2, w_in_2, q_norm_w_2, k_norm_w_2, sinks_2, w_attn_proj_2, A_re_2,
    A_im_2, log_dt_2, B_re_2, B_im_2, C_re_2, C_im_2, D_skip_2, w_glu_2, b_glu_2, w_ssm_proj_2,
    w_out_2,
):
    x = first_block(
        x, norm_mix, w_in, conv_dw, conv_b, conv_ln_g, conv_ln_b, shift_mu, w0, w_lora_up, a0,
        a_lora_up, g_lora_up, k_k, k_a, r_k, gn_g, gn_b, w_out, norm_ffn, router_group_w,
        router_group_b, router_expert_w, router_expert_b, expert_w_gate, expert_w_up,
        expert_w_down, norm_final,
    )
    return second_block(
        x, norm_w_2, w_in_2, q_norm_w_2, k_norm_w_2, sinks_2, w_attn_proj_2, A_re_2, A_im_2,
        log_dt_2, B_re_2, B_im_2, C_re_2, C_im_2, D_skip_2, w_glu_2, b_glu_2, w_ssm_proj_2,
        w_out_2,
    )


_drawn_inputs = setup_inputs


def setup_inputs(seed=0):
    import zlib

    import numpy as np

    out = dict(_drawn_inputs(seed))
    spreads = {}
    factors = {'conv_ln_b': 3.121,
     'w_lora_up': 4.907,
     'k_k': 3.623,
     'gn_g': 3.386,
     'gn_b': 3.27,
     'router_group_b': 6.141,
     'router_expert_b': 5.189,
     'norm_final': 2.785,
     'norm_w_2': 8.0,
     'q_norm_w_2': 8.0,
     'k_norm_w_2': 8.0,
     'sinks_2': 30.418,
     'A_re_2': 64.0,
     'A_im_2': 64.0,
     'log_dt_2': 64.0,
     'B_re_2': 64.0,
     'B_im_2': 64.0,
     'C_re_2': 64.0,
     'C_im_2': 64.0,
     'b_glu_2': 53.397}
    for name, (base, spread) in spreads.items():
        noise = np.random.default_rng([zlib.crc32(name.encode()), seed]).standard_normal(out[name].shape)
        drawn = base * np.exp(spread * noise) if base else spread * noise
        out[name] = __import__('jax').numpy.asarray(drawn.astype(out[name].dtype))
    for name, factor in factors.items():
        out[name] = (out[name] * factor).astype(out[name].dtype)
    return out
```

```python
import math
from contextlib import ExitStack

import numpy as np
import concourse.bass as bass
from concourse import mybir

F32 = mybir.dt.float32
I32 = mybir.dt.int32
U32 = mybir.dt.uint32
ALU = mybir.AluOpType
ACT = mybir.ActivationFunctionType
AX = mybir.AxisListType

P = 128
T = 512
TT = T // P
D = 2048
KD = D // P
BANKS = 8
QUARTERS = 4


class Steps:

    def __init__(self, eng, sem, base=0):
        self.eng, self.sem, self.base, self.n = eng, sem, base, 0

    def did(self, instruction):
        instruction.then_inc(self.sem, 1)
        self.n += 1
        return self.n

    def wait(self, n=None):
        self.eng.wait_ge(self.sem, self.base + (self.n if n is None else n))


class Scope:

    spent = []

    def __init__(self, nc, name):
        self.nc, self.name, self.stack = nc, name, ExitStack()

    def __enter__(self):
        return self

    def __exit__(self, *error):
        return self.stack.__exit__(*error)

    def sb(self, name, shape, dt=F32):
        return self.stack.enter_context(self.nc.sbuf_tensor(f"{self.name}_{name}", shape, dt))

    def ps(self, name, shape, dt=F32):
        return self.stack.enter_context(self.nc.psum_tensor(f"{self.name}_{name}", shape, dt))

    def sem(self, name):
        semaphore = self.nc.alloc_semaphore(name=f"{self.name}_{name}")
        Scope.spent.append(semaphore)
        return semaphore

    def banks(self, n=BANKS):
        return [self.ps(f"bank{i}", [P, T]) for i in range(n)]


def clear_semaphores(nc):
    nc.clear_and_free_semaphores(Scope.spent)
    Scope.spent = []
    nc.all_engine_barrier()


def constants(nc, ident, ones, block_ones):
    with Scope(nc, "constants") as s, nc.Block() as block:
        filled = s.sem("filled")

        @block.vector
        def _(dve):
            dve.memset(ident[:, :], 0.0).then_inc(filled, 1)
            dve.memset(ones[:, :], 1.0).then_inc(filled, 1)
            dve.memset(block_ones[:, :], 0.0).then_inc(filled, 1)
            dve.wait_ge(filled, 3)
            dve.memset(block_ones[0:64, 0:64], 1.0).then_inc(filled, 1)
            dve.memset(block_ones[64:128, 64:128], 1.0).then_inc(filled, 1)

        @block.gpsimd
        def _(pool):
            pool.wait_ge(filled, 5)
            pool.affine_select(out=ident[:, :], in_=ident[:, :], compare_op=ALU.not_equal, fill=1.0,
                               base=0, pattern=[[-1, P]], channel_multiplier=1).then_inc(filled, 1)
            pool.wait_ge(filled, 6)


def load_columns(nc, ident, rows, columns):
    n = columns.shape[1]
    with Scope(nc, f"columns_{columns.name}") as s:
        staged = s.sb("staged", [n, P])
        turned = s.ps("turned", [P, n])
        cleared, loaded, transposed, copied = s.sem("cleared"), s.sem("loaded"), s.sem("transposed"), s.sem("copied")
        with nc.Block() as block:
            @block.vector
            def _(dve):
                dve.memset(staged[:, :], 0.0).then_inc(cleared, 1)
                dve.wait_ge(transposed, 1)
                dve.tensor_copy(columns[:, :], turned[:, :]).then_inc(copied, 1)

            @block.sync
            def _(sp):
                sp.wait_ge(cleared, 1)
                for view, at, first in rows:
                    sp.dma_start(staged[at:at + view.shape[0], first:first + view.shape[1]], view).then_inc(loaded, 16)

            @block.tensor
            def _(pe):
                pe.wait_ge(loaded, 16 * len(rows))
                pe.transpose(turned[:, :], staged[:, :], ident[0:n, 0:n]).then_inc(transposed, 1)


def norm_transpose(nc, name, rows, gain, ident, out_T, eps, rows_out=None):
    scaled = rows if rows_out is None else rows_out
    with Scope(nc, name) as s:
        square = s.sb("square", [P, D])
        stat = s.sb("stat", [P, TT])
        root = s.sb("root", [P, TT])
        inv = s.sb("inv", [P, TT])
        bank = s.banks(4)
        squared, averaged, rooted, inverted, scaled_rows, turned, evacuated = (
            s.sem(n) for n in ("squared", "averaged", "rooted", "inverted", "scaled_rows", "turned", "evacuated"))
        with nc.Block() as block:
            @block.scalar
            def _(act):
                for t in range(TT):
                    act.activation(square[:, :], rows[:, t, :], ACT.Square,
                                   accum_out=stat[:, t:t + 1]).then_inc(squared, 1)
                    act.wait_ge(squared, t + 1)
                act.wait_ge(averaged, 1)
                act.activation(root[:, :], root[:, :], ACT.Sqrt).then_inc(rooted, 1)

            @block.vector
            def _(dve):
                dve.wait_ge(squared, TT)
                dve.tensor_scalar(root[:, :], stat[:, :], 1.0 / D, eps, ALU.mult, ALU.add).then_inc(averaged, 1)
                dve.wait_ge(rooted, 1)
                dve.reciprocal(inv[:, :], root[:, :]).then_inc(inverted, 1)
                dve.wait_ge(inverted, 1)
                for t in range(TT):
                    dve.tensor_scalar(scaled[:, t, :], rows[:, t, :], inv[:, t:t + 1], None,
                                      ALU.mult).then_inc(scaled_rows, 1)
                for k in range(KD):
                    dve.wait_ge(turned, k + 1)
                    dve.tensor_scalar(out_T[:, k, :], bank[k % 4][:, :], gain[:, k:k + 1], None,
                                      ALU.mult).then_inc(evacuated, 1)

            @block.tensor
            def _(pe):
                pe.wait_ge(scaled_rows, TT)
                for k in range(KD):
                    if k >= 4:
                        pe.wait_ge(evacuated, k - 3)
                    for t in range(TT):
                        mm = pe.transpose(bank[k % 4][:, t * P:(t + 1) * P],
                                          scaled[:, t, k * P:(k + 1) * P], ident[:, :])
                    mm.then_inc(turned, 1)


class Gemm:

    def __init__(self, nc, s, ring, left, KT, pairs, weights, channels, odd=False):
        self.nc, self.left, self.KT, self.pairs = nc, left, KT, pairs
        self.ring, self.weights, self.channels, self.odd = ring, weights, channels, odd
        self.bank = s.banks()
        self.arrived = [[s.sem(f"arrived{i}_{q}") for q in range(QUARTERS)] for i in range(2)]
        self.used = [s.sem(f"used{i}") for i in range(2)]
        self.product = s.sem("product")
        self.bank_free = s.sem("bank_free")

    def load_panel(self, sp, panel, slot, use):
        kq = self.KT // QUARTERS
        for q in range(QUARTERS):
            if use is not None and q < QUARTERS - 1:
                sp.wait_ge(self.used[slot], (QUARTERS - 1) * use + q + 1)
            elif use is not None:
                sp.wait_ge(self.product, BANKS * use + 4 * slot + 4)
            sp.dma_start(self.ring[slot][:, q * kq:(q + 1) * kq, :],
                         self.weights(panel).rearrange("(k p) c -> p k c", p=P)[:, q * kq:(q + 1) * kq, :]
                         ).then_inc(self.arrived[slot][q], 16)

    def sync(self, sp):
        self.load_panel(sp, 0, 0, None)
        if self.pairs:
            self.load_panel(sp, 1, 1, None)
        if self.pairs > 1:
            with sp.Fori(0, self.pairs - 1) as i:
                for slot in range(2):
                    self.load_panel(sp, 2 * i + 2 + slot, slot, i)
        if self.odd:
            self.load_panel(sp, 2 * self.pairs, 0, self.pairs - 1)

    def turn(self, pe, i, slots):
        kq = self.KT // QUARTERS
        for slot in slots:
            w = self.ring[slot]
            for q in range(QUARTERS):
                pe.wait_ge(self.arrived[slot][q], 16 * i + 16)
                for sub in range(4):
                    b = 4 * slot + sub
                    if q == 0:
                        pe.wait_ge(self.bank_free, BANKS * i + b + 1)
                    cut = slice(sub * P, (sub + 1) * P)
                    for k in range(q * kq, (q + 1) * kq):
                        lhs, rhs = ((w[:, k, cut], self.left[:, k, :]) if self.channels else
                                    (self.left[:, k, cut], w[:, k, :]))
                        mm = pe.matmul(self.bank[b][:, :], lhs, rhs, start=(k == 0), stop=(k == self.KT - 1))
                    if q < QUARTERS - 1 and sub == 3:
                        mm.then_inc(self.used[slot], 1)
                    if q == QUARTERS - 1:
                        mm.then_inc(self.product, 1)

    def tensor(self, pe):
        pe.sem_inc(self.bank_free, BANKS)
        if self.pairs:
            with pe.Fori(0, self.pairs) as i:
                self.turn(pe, i, (0, 1))
        if self.odd:
            self.turn(pe, self.pairs, (0,))

    def drain(self, eng, first, last, copy):
        with eng.Fori(first, last) as i:
            self.drain_turn(eng, i, (0, 1), copy)

    def drain_turn(self, eng, i, slots, copy):
        for slot in slots:
            for sub in range(4):
                b = 4 * slot + sub
                eng.wait_ge(self.product, BANKS * i + b + 1)
                copy(self.bank[b], 2 * i + slot, sub, b, i)


def load_rows(nc, name, view, rows):
    with Scope(nc, name) as s:
        loaded = s.sem("loaded")
        with nc.Block() as block:
            @block.sync
            def _(sp):
                sp.dma_start(rows[:, :, :], view.rearrange("(t p) d -> p t d", p=P)).then_inc(loaded, 16)
                sp.wait_ge(loaded, 16)


def load_taps(nc, conv_dw, ident, taps):
    n, width = conv_dw.shape
    with Scope(nc, "taps") as s:
        staged = s.sb("staged", [n, width])
        turned = s.ps("turned", [P, width // P, 32])
        loaded, transposed, copied = s.sem("loaded"), s.sem("transposed"), s.sem("copied")
        with nc.Block() as block:
            @block.sync
            def _(sp):
                sp.dma_start(staged[:, :], conv_dw).then_inc(loaded, 16)

            @block.tensor
            def _(pe):
                pe.wait_ge(loaded, 16)
                for t in range(width // P):
                    mm = pe.transpose(turned[:, t, 0:n], staged[:, t * P:(t + 1) * P], ident[0:n, 0:n])
                mm.then_inc(transposed, 1)

            @block.vector
            def _(dve):
                dve.wait_ge(transposed, 1)
                dve.tensor_copy(taps[:, :, :], turned[:, :, 0:n]).then_inc(copied, 1)


def vector_rows(vector):
    n = vector.shape[0]
    whole = n // P
    views = []
    if whole:
        views.append(vector[0:whole * P].rearrange("(r c) -> r c", c=P))
    if n % P:
        views.append(vector[whole * P:n].rearrange("(r c) -> r c", r=1))
    return views


class Columns:

    def __init__(self, nc, s, name, vectors, twice=()):
        self.at, self.rows, n = {}, [], 0
        for key, vector in vectors:
            first = n
            for view in vector_rows(vector):
                self.rows.append((view, n, 0))
                n += view.shape[0]
            self.at[key] = (first, n)
        for key, vector in twice:
            for first in (0, P // 2):
                self.rows.append((vector.unsqueeze(0), n, first))
            n += 1
            self.at[key] = (n - 1, n)
        self.tile = s.sb(name, [P, n])

    def __getitem__(self, key):
        a, b = self.at[key]
        return self.tile[:, a:b]


CW = 31
CT = 8
RT = 27
TAIL = 288


def project_in(nc, w_in, u_T, ring, conv_T, rwkv_T, taps, conv_bias, mu):
    with Scope(nc, "project_in") as s:
        g = Gemm(nc, s, ring, u_T, KD, 5, lambda panel: w_in[:, bass.ds(panel * T, T)], channels=True)
        gated = s.sb("gated", [P, 2, CW - 1 + T])
        change = s.sb("change", [P, T])
        tail_in, cleared, conv_step, mix_step, gap = (
            s.sem(n) for n in ("tail_in", "cleared", "conv_step", "mix_step", "gap"))
        last = BANKS * 5
        with nc.Block() as block:
            @block.sync
            def _(sp):
                g.sync(sp)
                sp.wait_ge(g.product, last - 4)
                sp.dma_start(ring[0][:, :, 0:TAIL],
                             w_in[:, 10 * T:10 * T + TAIL].rearrange("(k p) c -> p k c", p=P)).then_inc(tail_in, 16)

            @block.tensor
            def _(pe):
                g.tensor(pe)
                pe.wait_ge(tail_in, 16)
                for sub, rows in enumerate((P, P, 32)):
                    pe.wait_ge(g.bank_free, last + sub + 1)
                    for k in range(KD):
                        mm = pe.matmul(g.bank[sub][0:rows, :], ring[0][:, k, sub * P:sub * P + rows],
                                       u_T[:, k, :], start=(k == 0), stop=(k == KD - 1))
                    mm.then_inc(g.product, 1)

            @block.scalar
            def _(act):
                act.wait_ge(cleared, 1)
                g.drain(act, 0, 1, lambda bank, panel, sub, b, i: act.activation(
                    conv_T[:, bass.ds(panel * 4 + sub, 1), :], bank[:, :], ACT.Copy).then_inc(g.bank_free, 1))
                g.drain(act, 1, 2, lambda bank, panel, sub, b, i: act.activation(
                    conv_T[:, bass.ds(panel * 4 + sub, 1), :], bank[:, :], ACT.Sigmoid).then_inc(g.bank_free, 1))
                g.drain(act, 2, 5, lambda bank, panel, sub, b, i: act.activation(
                    rwkv_T[:, bass.ds(panel * 4 + sub - 2 * CT, 1), 1:1 + T], bank[:, :], ACT.Copy).then_inc(g.bank_free, 1))
                for sub, rows in enumerate((P, P, 32)):
                    act.wait_ge(g.product, last + sub + 1)
                    act.activation(rwkv_T[0:rows, 24 + sub, 1:1 + T], g.bank[sub][0:rows, :],
                                   ACT.Copy).then_inc(g.bank_free, 1)

            @block.vector
            def _(dve):
                dve.memset(rwkv_T[:, :, 0:1], 0.0).then_inc(cleared, 1)
                dve.memset(gated[:, :, 0:CW - 1], 0.0).then_inc(cleared, 1)
                dve.wait_ge(cleared, 2)
                dve.wait_ge(g.bank_free, BANKS + 2 * BANKS)
                per = 2 * (1 + CW)
                with dve.Fori(0, CT // 2) as i:
                    steps = Steps(dve, conv_step, i * per)
                    for a in range(2):
                        steps.did(dve.tensor_tensor(
                            gated[:, a:a + 1, CW - 1:], conv_T[:, bass.ds(2 * i + a, 1), :],
                            conv_T[:, bass.ds(CT + 2 * i + a, 1), :], ALU.mult))
                    for tap in range(CW):
                        for a in range(2):
                            steps.wait(steps.n - 1)
                            acc = conv_T[:, bass.ds(2 * i + a, 1), :]
                            at = gated[:, a:a + 1, tap:tap + T]
                            w = taps[:, bass.ds(2 * i + a, 1), tap]
                            if tap == 0:
                                steps.did(dve.tensor_scalar(acc, at, w, conv_bias[:, bass.ds(2 * i + a, 1)],
                                                            ALU.mult, ALU.add))
                            else:
                                steps.did(dve.scalar_tensor_tensor(out=acc, in0=at, scalar=w, in1=acc,
                                                                   op0=ALU.mult, op1=ALU.add))
                    assert steps.n == per
                    steps.wait()

                def mix(steps, tile, rows):
                    steps.wait()
                    steps.did(dve.tensor_tensor(change[0:rows, :], rwkv_T[0:rows, tile, 0:T],
                                                rwkv_T[0:rows, tile, 1:1 + T], ALU.subtract))
                    steps.wait()
                    steps.did(dve.scalar_tensor_tensor(
                        out=rwkv_T[0:rows, tile, 1:1 + T], in0=change[0:rows, :], scalar=mu[0:rows, tile],
                        in1=rwkv_T[0:rows, tile, 1:1 + T], op0=ALU.mult, op1=ALU.add))

                with dve.Fori(0, 3 * CT) as i:
                    dve.wait_ge(g.bank_free, i + (BANKS + 2 * CT + 1))
                    steps = Steps(dve, mix_step, 2 * i + 1)
                    mix(steps, bass.ds(i, 1), P)
                steps = Steps(dve, mix_step, 6 * CT + 1)
                for sub, rows in enumerate((P, P, 32)):
                    dve.wait_ge(g.bank_free, BANKS + last + sub + 1)
                    mix(steps, slice(24 + sub, 25 + sub), rows)
                steps.wait()

            @block.gpsimd
            def _(pool):
                pool.sem_inc(mix_step, 1)


def conv_norm(nc, conv_T, ones, ln_g, ln_b):
    n = CT * P
    with Scope(nc, "conv_norm") as s:
        square = s.sb("square", [P, CT, T])
        var = s.sb("var", [P, T])
        rstd = s.sb("rstd", [P, T])
        bank = s.banks(2)
        summed, centred, squared, var_summed, var_ready, rooted, inverted, scaled, done = (
            s.sem(x) for x in ("summed", "centred", "squared", "var_summed", "var_ready", "rooted", "inverted", "scaled", "done"))
        with nc.Block() as block:
            @block.tensor
            def _(pe):
                for t in range(CT):
                    mm = pe.matmul(bank[0][:, :], ones[:, :], conv_T[:, t, :], start=(t == 0), stop=(t == CT - 1))
                mm.then_inc(summed, 1)
                for t in range(CT):
                    pe.wait_ge(squared, t + 1)
                    mm = pe.matmul(bank[1][:, :], ones[:, :], square[:, t, :], start=(t == 0), stop=(t == CT - 1))
                mm.then_inc(var_summed, 1)

            @block.vector
            def _(dve):
                dve.wait_ge(summed, 1)
                for t in range(CT):
                    dve.scalar_tensor_tensor(out=conv_T[:, t, :], in0=bank[0][:, :], scalar=-1.0 / n,
                                             in1=conv_T[:, t, :], op0=ALU.mult, op1=ALU.add).then_inc(centred, 1)
                dve.wait_ge(var_summed, 1)
                dve.tensor_scalar(var[:, :], bank[1][:, :], 1.0 / n, 1e-5, ALU.mult, ALU.add).then_inc(var_ready, 1)
                dve.wait_ge(rooted, 1)
                dve.reciprocal(rstd[:, :], var[:, :]).then_inc(inverted, 1)
                dve.wait_ge(inverted, 1)
                dve.wait_ge(centred, CT)
                for t in range(CT):
                    dve.tensor_tensor(conv_T[:, t, :], conv_T[:, t, :], rstd[:, :], ALU.mult).then_inc(scaled, 1)

            @block.scalar
            def _(act):
                for t in range(CT):
                    act.wait_ge(centred, t + 1)
                    act.activation(square[:, t, :], conv_T[:, t, :], ACT.Square).then_inc(squared, 1)
                act.wait_ge(var_ready, 1)
                act.activation(var[:, :], var[:, :], ACT.Sqrt).then_inc(rooted, 1)
                for t in range(CT):
                    act.wait_ge(scaled, t + 1)
                    act.activation(conv_T[:, t, :], conv_T[:, t, :], ACT.Silu, bias=ln_b[:, t:t + 1],
                                   scale=ln_g[:, t:t + 1]).then_inc(done, 1)
                act.wait_ge(done, CT)


C = 64
NC = T // C
LEVELS = 5


def chunk_masks(nc, block_ones, lower, upper, upper_incl, first, level):
    with Scope(nc, "chunk_masks") as s:
        row = s.sb("row", [P, P], I32)
        col = s.sb("col", [P, P], I32)
        differ = s.sb("differ", [P, P], I32)
        shifted = s.sb("shifted", [P, P], I32)
        same = s.sb("same", [P, P])
        counted, step = s.sem("counted"), s.sem("step")
        with nc.Block() as block:
            @block.gpsimd
            def _(pool):
                pool.iota(row[:, :], [[0, P]], base=0, channel_multiplier=1).then_inc(counted, 1)
                pool.iota(col[:, :], [[1, P]], base=0, channel_multiplier=0).then_inc(counted, 1)

            @block.vector
            def _(dve):
                steps = Steps(dve, step)
                dve.wait_ge(counted, 2)
                steps.did(dve.tensor_tensor(lower[:, :], row[:, :], col[:, :], ALU.is_gt))
                steps.did(dve.tensor_tensor(upper[:, :], row[:, :], col[:, :], ALU.is_lt))
                steps.did(dve.tensor_tensor(upper_incl[:, :], row[:, :], col[:, :], ALU.is_le))
                steps.did(dve.tensor_tensor(differ[:, :], row[:, :], col[:, :], ALU.bitwise_xor))
                steps.wait()
                for m in (lower, upper, upper_incl):
                    steps.did(dve.tensor_tensor(m[:, :], m[:, :], block_ones[:, :], ALU.mult))
                for l in range(LEVELS + 1):
                    steps.wait()
                    steps.did(dve.tensor_scalar(shifted[:, :], differ[:, :], l, None, ALU.logical_shift_right))
                    steps.wait()
                    steps.did(dve.tensor_scalar(same[:, :], shifted[:, :], 1.0, None, ALU.is_equal))
                    steps.wait()
                    if l == 0:
                        steps.did(dve.tensor_tensor(first[:, 0, :], same[:, :], lower[:, :], ALU.mult))
                        steps.did(dve.tensor_tensor(first[:, 1, :], same[:, :], upper[:, :], ALU.mult))
                    else:
                        steps.did(dve.tensor_tensor(level[:, l - 1, :], same[:, :], lower[:, :], ALU.mult))
                steps.wait()


def rwkv(nc, a, cols, ident, block_ones, rwkv_T, mixed_T):
    names = ["lora", "lora_copied", "sig", "logs", "exps", "keys", "keys_sq", "keys_sum", "keys_root", "chans",
             "bonus_in", "bonus_sum", "turned", "tokens", "scores", "masked", "t_init", "w_mm", "w_ev", "t_mm", "t_ev",
             "x_mm", "x_ev", "gh_mm", "gh_ev", "mt_mm", "mt_ev", "q_mm", "q_ev", "f_mm", "state", "s_masked",
             "y_mm", "y_ev", "mean_mm", "centred", "y_sq", "var_mm", "var", "root",
             "normed", "affine", "pair_done", "dve_step", "gate_ev", "pre_step", "kept", "passed"]
    with Scope(nc, "rwkv") as s:
        sem = {n: s.sem(n) for n in names}
        lower, upper, upper_incl = (s.sb(n, [P, P]) for n in ("lower", "upper", "upper_incl"))
        first, level = s.sb("first", [P, 2, P]), s.sb("level", [P, LEVELS, P])
        carry = s.sb("carry", [P, T])
        lora_up = s.sb("lora_up", [P, CT * P])
        g_up = s.sb("g_up", [P, 2, CT * P])
        g_in = s.sb("g_in", [P, 2, T])
        chunk_masks(nc, block_ones, lower, upper, upper_incl, first, level)
        loaded, ready, ranks = s.sem("loaded"), s.sem("ready"), s.sem("ranks")
        with nc.Block() as block:
            @block.sync
            def _(sp):
                sp.dma_start(lora_up[0:C, :], a["w_lora_up"][0]).then_inc(loaded, 16)
                sp.dma_start(lora_up[C:P, :], a["a_lora_up"][0]).then_inc(loaded, 16)
                sp.dma_start(g_up[:, 0, :], a["g_lora_up"][0][0:P, :]).then_inc(loaded, 16)
                sp.dma_start(g_up[0:32, 1, :], a["g_lora_up"][0][P:P + 32, :]).then_inc(loaded, 16)
                sp.wait_ge(loaded, 64)

            @block.vector
            def _(dve):
                dve.memset(carry[:, :], 1.0).then_inc(ready, 1)
                dve.wait_ge(ready, 1)
                dve.memset(carry[:, :].rearrange("p (c t) -> p c t", t=C)[:, :, 0:1], 0.0).then_inc(ready, 1)
                dve.wait_ge(ready, 2)

            @block.scalar
            def _(act):
                act.activation(g_in[:, 0, :], rwkv_T[:, 25, 1:1 + T], ACT.Sigmoid).then_inc(ranks, 1)
                act.activation(g_in[0:32, 1, :], rwkv_T[0:32, 26, 1:1 + T], ACT.Sigmoid).then_inc(ranks, 1)
                act.activation(rwkv_T[0:C, 24, 1:1 + T], rwkv_T[0:C, 24, 1:1 + T], ACT.Tanh).then_inc(ranks, 1)
                act.wait_ge(ranks, 3)
        w_in, a_in = rwkv_T[0:C, 24, 1:1 + T], rwkv_T[C:P, 24, 1:1 + T]

        def sbt(n):
            return s.sb(n, [P, T])

        lora_now, g_now = s.sb("lora_now", [P, P]), s.sb("g_now", [P, 2, P])
        log_w, rate, gate, cum = (sbt(n) for n in ("log_w", "rate", "gate", "cum"))
        e_cum, e_inv, e_before, e_rest = (sbt(n) for n in ("e_cum", "e_inv", "e_before", "e_rest"))
        kk, k2, bonus = sbt("kk"), sbt("k2"), sbt("bonus")
        a_c, r_c, b_c, k_c, bh_c, kh_c, v_c = (sbt(n) for n in ("a_c", "r_c", "b_c", "k_c", "bh_c", "kh_c", "v_c"))
        a_t, bh_t, kh_t, v_t = toks = [sbt(n) for n in ("a_t", "bh_t", "kh_t", "v_t")]
        akT, NT, rbT, rkT, Tm, Tt, W = (s.sb(n, [P, 2, T]) for n in ("akT", "NT", "rbT", "rkT", "Tm", "Tt", "W"))
        G, H, y, tmp = (sbt(n) for n in ("G", "H", "y", "tmp"))
        Q = akT[:, 0, :]
        X = y
        pre_tmp = sbt("pre_tmp")
        kept = r_k, e_k, gate_k, bonus_k = [sbt(n) for n in ("r_k", "e_k", "gate_k", "bonus_k")]
        prepared = (r_c, e_cum, gate, bonus)
        S = s.sb("S", [P, NC, P])
        MT = W[:, :, :].rearrange("p h (c k) -> p (h c) k", k=P)
        S_own = Tm[:, :, :].rearrange("p h (c k) -> p (h c) k", k=P)
        bank = s.banks()

        def chunks(x):
            return x[:, :].rearrange("p (c t) -> p c t", t=C)

        def wide(mask, n):
            return mask.unsqueeze(1).broadcast_to([P, n, P])

        def quads(x):
            return x.rearrange("p (c t) -> p c t", t=P)

        def tok(x, h, cp):
            return x[:, (cp * 2 + h) * C:(cp * 2 + h) * C + C]

        def tok_half(x, c):
            return x[(c % 2) * C:(c % 2) * C + C, (c // 2) * P:(c // 2) * P + P]

        def sq(x, h, cp):
            return x[:, h, cp * P:(cp + 1) * P]

        r_in = lambda j: rwkv_T[:, bass.ds(j, 1), 1:1 + T]
        k_in = lambda j: rwkv_T[:, bass.ds(CT + j, 1), 1:1 + T]
        v_in = lambda j: rwkv_T[:, bass.ds(2 * CT + j, 1), 1:1 + T]
        turn_bank = (5, 6, 7, 0)
        score = (("N^T", b_c, a_c, (2, 3)), ("A_ak^T", k_c, a_c, (1, 4)), ("N", a_c, b_c, (5, 6)),
                 ("A_rb^T", b_c, r_c, (7, 0)), ("A_rk^T", k_c, r_c, (2, 3)))
        w_bank, tt_bank, tm_bank, f_bank = (1, 4), (5, 6), (7, 0), (7, 0)
        per_t = 2 * (2 * LEVELS - 1)

        with nc.Block() as block:
            @block.tensor
            def _(pe):
                def prepare(j, part):
                    wait = lambda n, per=1, k=1: pe.wait_ge(sem[n], j * per + k)
                    done = lambda mm, n: mm.then_inc(sem[n], 1)
                    if part == 0:
                        wait("lora_copied", 3, 3)
                        done(pe.matmul(bank[2][:, :], lora_now[0:C, :], w_in, start=True, stop=True), "lora")
                        done(pe.matmul(bank[3][:, :], lora_now[C:P, :], a_in, start=True, stop=True), "lora")
                    elif part == 1:
                        wait("sig", 2, 2)
                        pe.matmul(bank[2][:, :], g_now[:, 0, :], g_in[:, 0, :], start=True, stop=False)
                        done(pe.matmul(bank[2][:, :], g_now[0:32, 1, :], g_in[0:32, 1, :], start=False, stop=True), "lora")
                        wait("keys_sq")
                        done(pe.matmul(bank[3][:, :], block_ones[:, :], pre_tmp[:, :], start=True, stop=True), "keys_sum")
                    else:
                        wait("gate_ev")
                        wait("bonus_in")
                        done(pe.matmul(bank[2][:, :], block_ones[:, :], bonus[:, :], start=True, stop=True), "bonus_sum")

                def pair(j, last):
                    wait = lambda n, per=1, k=1: pe.wait_ge(sem[n], j * per + k)
                    done = lambda mm, n: mm.then_inc(sem[n], 1)
                    wait("bonus_sum", 2, 2)
                    wait("var")
                    wait("chans", 7, 7)
                    for b, x in zip(turn_bank, (a_c, bh_c, kh_c, v_c)):
                        for cp in range(4):
                            mm = pe.transpose(bank[b][:, cp * P:(cp + 1) * P], x[:, cp * P:(cp + 1) * P], ident[:, :])
                        done(mm, "turned")
                    for i, (_, lhs, rhs, banks) in enumerate(score):
                        if i == 2:
                            wait("tokens", 4, 2)
                        if i == 3:
                            wait("tokens", 4, 4)
                        if i == 4:
                            wait("masked", 8, 2)
                        for h in range(2):
                            half = slice(h * C, h * C + C)
                            for cp in range(4):
                                cut = slice(cp * P, cp * P + P)
                                mm = pe.matmul(bank[banks[h]][:, cut], lhs[half, cut], rhs[half, cut], start=True, stop=True)
                            done(mm, "scores")
                    for l in range(LEVELS):
                        if l == 1:
                            wait("masked", 8, 8)
                        if 1 <= l <= 3 and not last:
                            prepare(j + 1, l - 1)
                        for h in range(2):
                            if l == 0:
                                wait("masked", 8, 4)
                                wait("t_init", 4, 2 * h + 2)
                            else:
                                wait("t_ev", per_t, 4 * (l - 1) + 2 * h + 2)
                            for cp in range(4):
                                mm = pe.matmul(bank[w_bank[h]][:, cp * P:(cp + 1) * P], sq(NT, h, cp), sq(Tm, h, cp),
                                               start=True, stop=True)
                            done(mm, "w_mm")
                        for h in range(2):
                            wait("w_ev", 2 * LEVELS, 2 * l + h + 1)
                            if l == 0:
                                wait("masked", 8, 6)
                            for cp in range(4):
                                mm = pe.matmul(bank[tt_bank[h]][:, cp * P:(cp + 1) * P], sq(W, h, cp), sq(Tt, h, cp),
                                               start=True, stop=True)
                            if l < LEVELS - 1:
                                for cp in range(4):
                                    mm = pe.matmul(bank[tm_bank[h]][:, cp * P:(cp + 1) * P], sq(Tt, h, cp), sq(W, h, cp),
                                                   start=True, stop=True)
                            done(mm, "t_mm")
                        if l == 3:
                            if not last:
                                pe.wait_ge(sem["keys_root"], j + 2)
                            for h in range(2):
                                for cp in range(4):
                                    mm = pe.matmul(tok(bank[3], h, cp), sq(akT, h, cp), tok(v_t, h, cp), start=True, stop=True)
                            done(mm, "x_mm")
                    wait("t_ev", per_t, per_t)
                    if not last:
                        pe.wait_ge(sem["bonus_sum"], 2 * j + 4)
                    for h in range(2):
                        for cp in range(4):
                            mm = pe.matmul(tok(bank[2], h, cp), sq(Tt, h, cp), tok(a_t, h, cp), start=True, stop=True)
                    done(mm, "gh_mm")
                    wait("x_ev")
                    for h in range(2):
                        for cp in range(4):
                            mm = pe.matmul(tok(bank[3], h, cp), sq(Tt, h, cp), tok(X, h, cp), start=True, stop=True)
                    done(mm, "gh_mm")
                    wait("gh_ev", 2, 1)
                    for c in range(NC):
                        mm = pe.matmul(bank[w_bank[c % 2]][:, (c // 2) * P:(c // 2) * P + P], tok_half(H, c),
                                       tok_half(bh_t, c), start=True, stop=True)
                    done(mm, "mt_mm")
                    for h in range(2):
                        for cp in range(4):
                            mm = pe.matmul(bank[5][h * C:h * C + C, cp * P:(cp + 1) * P], tok(H, h, cp), sq(rbT, h, cp),
                                           start=True, stop=True)
                    done(mm, "q_mm")
                    wait("gh_ev", 2, 2)
                    for c in range(NC - 1):
                        out = bank[f_bank[c % 2]][:, (c // 2) * P:(c // 2) * P + P]
                        pe.matmul(out, tok_half(kh_t, c), tok_half(v_t, c), start=(c < 2), stop=False,
                                  skip_group_check=True)
                        mm = pe.matmul(out, tok_half(bh_t, c), tok_half(G, c), start=False, stop=False,
                                       skip_group_check=True)
                    done(mm, "f_mm")
                    wait("mt_ev", 2, 2)
                    for c in range(1, NC - 1):
                        wait("state", NC - 1, c)
                        done(pe.matmul(bank[f_bank[c % 2]][:, (c // 2) * P:(c // 2) * P + P], MT[:, c, :], S[:, c, :],
                                       start=False, stop=True, skip_group_check=True), "f_mm")
                    wait("q_ev")
                    wait("s_masked")
                    for cp in range(4):
                        for h in range(2):
                            out = bank[6][h * C:h * C + C, cp * P:(cp + 1) * P]
                            pe.matmul(out, tok(G, h, cp), sq(rbT, h, cp), start=True, stop=False, skip_group_check=True)
                            pe.matmul(out, tok(v_t, h, cp), sq(rkT, h, cp), start=False, stop=False, skip_group_check=True)
                        for c in (2 * cp, 2 * cp + 1):
                            mm = pe.matmul(bank[6][:, c * C:c * C + C], S_own[:, c, :], Q[:, c * C:c * C + C],
                                           start=False, stop=True, skip_group_check=True)
                    done(mm, "y_mm")
                    wait("y_ev")
                    done(pe.matmul(bank[2][:, :], block_ones[:, :], y[:, :], start=True, stop=True), "mean_mm")
                    wait("y_sq")
                    done(pe.matmul(bank[3][:, :], block_ones[:, :], tmp[:, :], start=True, stop=True), "var_mm")

                for part in range(3):
                    prepare(0, part)
                with pe.Fori(0, CT - 1) as j:
                    pair(j, False)
                pair(CT - 1, True)

            @block.scalar
            def _(act):
                def prepare(j, part):
                    wait = lambda n, per=1, k=1: act.wait_ge(sem[n], j * per + k)
                    done = lambda ins, n: ins.then_inc(sem[n], 1)
                    col = lambda key: cols[key][:, bass.ds(j, 1)]
                    if part == 0:
                        wait("lora", 3, 1)
                        done(act.activation(log_w[:, :], bank[2][:, :], ACT.Sigmoid, bias=col("w0")), "sig")
                        wait("lora", 3, 2)
                        done(act.activation(rate[:, :], bank[3][:, :], ACT.Sigmoid, bias=col("a0")), "sig")
                        wait("keys")
                        done(act.activation(pre_tmp[:, :], kk[:, :], ACT.Square), "keys_sq")
                        wait("kept", 4, 4)
                        wait("lora", 3, 3)
                        done(act.activation(gate[:, :], bank[2][:, :], ACT.Copy), "gate_ev")
                    elif part == 1:
                        wait("logs", 3, 3)
                        done(act.activation(e_cum[:, :], cum[:, :], ACT.Exp), "exps")
                        done(act.activation(e_inv[:, :], cum[:, :], ACT.Exp, scale=-1.0), "exps")
                        done(act.activation(e_before[:, :], e_before[:, :], ACT.Exp), "exps")
                        done(act.activation(e_rest[:, :], e_rest[:, :], ACT.Exp), "exps")
                        wait("keys_sum")
                        done(act.activation(pre_tmp[:, :], bank[3][:, :], ACT.Sqrt), "keys_root")

                def pair(j, last):
                    wait = lambda n, per=1, k=1: act.wait_ge(sem[n], j * per + k)
                    done = lambda ins, n: ins.then_inc(sem[n], 1)
                    col = lambda key: cols[key][:, bass.ds(j, 1)]
                    for i, x in enumerate(toks):
                        wait("turned", 4, i + 1)
                        done(act.activation(x[:, :], bank[turn_bank[i]][:, :], ACT.Copy), "tokens")
                    if not last:
                        prepare(j + 1, 0)
                        prepare(j + 1, 1)
                    wait("x_mm")
                    done(act.activation(X[:, :], bank[3][:, :], ACT.Copy), "x_ev")
                    wait("gh_mm", 2, 1)
                    done(act.activation(H[:, :], bank[2][:, :], ACT.Copy), "gh_ev")
                    wait("gh_mm", 2, 2)
                    done(act.activation(G[:, :], bank[3][:, :], ACT.Copy), "gh_ev")
                    wait("y_mm")
                    done(act.activation(y[:, :], bank[6][:, :], ACT.Copy), "y_ev")
                    wait("centred")
                    done(act.activation(tmp[:, :], y[:, :], ACT.Square), "y_sq")
                    wait("var", 1, 2)
                    done(act.activation(tmp[:, :], tmp[:, :], ACT.Sqrt), "root")
                    wait("normed")
                    done(act.activation(y[:, :], y[:, :], ACT.Identity, bias=col("gn_b"), scale=col("gn_g")), "affine")

                prepare(0, 0)
                prepare(0, 1)
                with act.Fori(0, CT - 1) as j:
                    pair(j, False)
                pair(CT - 1, True)

            @block.gpsimd
            def _(pool):
                def columns(j, first=False):
                    if not first:
                        pool.wait_ge(sem["lora"], 3 * j)
                    for out, src in ((lora_now[:, :], lora_up[:, bass.ds(j * P, P)]),
                                     (g_now[:, 0, :], g_up[:, 0, bass.ds(j * P, P)]),
                                     (g_now[0:32, 1, :], g_up[0:32, 1, bass.ds(j * P, P)])):
                        pool.tensor_copy(out, src).then_inc(sem["lora_copied"], 1)

                def keep(j):
                    pool.wait_ge(sem["pair_done"], j + 1)
                    pool.wait_ge(sem["exps"], 4 * j + 4)
                    pool.wait_ge(sem["gate_ev"], j + 1)
                    pool.wait_ge(sem["chans"], 7 * j + 7)
                    pool.wait_ge(sem["bonus_sum"], 2 * j + 2)
                    pool.sem_inc(sem["passed"], 1)
                    for out, src in zip(kept, prepared):
                        pool.tensor_copy(out[:, :], src[:, :]).then_inc(sem["kept"], 1)

                pool.sem_inc(sem["var"], 1)
                pool.sem_inc(sem["kept"], 4)
                columns(0, first=True)
                with pool.Fori(0, CT - 1) as j:
                    keep(j)
                    columns(j + 1)
                keep(CT - 1)

            @block.vector
            def _(dve):
                dve.sem_inc(sem["pair_done"], 1)

                def prepare(j, part):
                    steps = Steps(dve, sem["pre_step"], j * PREPARE_STEPS)
                    steps.n = PREPARED_BEFORE[part]
                    wait = lambda n, per=1, k=1: dve.wait_ge(sem[n], j * per + k)
                    col = lambda key: cols[key][:, bass.ds(j, 1)]
                    tt = lambda out, x, y_, op: dve.tensor_tensor(out, x, y_, op)
                    full = lambda x: x[:, :]
                    sig = lambda ins, n: ins.then_inc(sem[n], 1)
                    if part == 0:
                        sig(dve.tensor_scalar(full(kk), k_in(j), col("k_k"), None, ALU.mult), "keys")
                    if part == 1:
                        wait("sig", 2, 2)
                        steps.did(dve.tensor_scalar(full(log_w), full(log_w), -math.exp(-0.5), None, ALU.mult))
                        steps.wait()
                        sig(dve.tensor_tensor_scan(full(cum), full(carry), full(log_w), 0.0, ALU.mult, ALU.add), "logs")
                        wait("logs", 3, 1)
                        sig(tt(full(e_before), full(cum), full(log_w), ALU.subtract), "logs")
                        sig(tt(chunks(e_rest), chunks(cum)[:, :, C - 1:C].broadcast_to([P, NC, C]), chunks(cum), ALU.subtract), "logs")
                    if part == 2:
                        steps.did(dve.tensor_scalar(full(k2), full(rate), -1.0, col("k_a"), ALU.add, ALU.mult))
                        steps.wait()
                        steps.did(dve.scalar_tensor_tensor(out=full(k2), in0=full(k2), scalar=1.0, in1=k_in(j),
                                                           op0=ALU.add, op1=ALU.mult))
                        steps.wait()
                        wait("kept", 4, 4)
                        sig(dve.scalar_tensor_tensor(out=full(bonus), in0=r_in(j), scalar=col("r_k"), in1=full(k2),
                                                     op0=ALU.mult, op1=ALU.mult), "bonus_in")
                    if part == 3:
                        wait("exps", 4, 4)
                        wait("kept", 4, 4)
                        sig(dve.tensor_copy(full(v_c), v_in(j)), "chans")
                        sig(tt(full(r_c), r_in(j), full(e_cum), ALU.mult), "chans")
                        sig(tt(full(k_c), full(k2), full(e_inv), ALU.mult), "chans")
                        sig(tt(full(kh_c), full(k2), full(e_rest), ALU.mult), "chans")
                    if part == 4:
                        wait("keys_root")
                        steps.did(dve.tensor_scalar(full(pre_tmp), full(pre_tmp), 1e-12, None, ALU.max))
                        steps.wait()
                        steps.did(dve.reciprocal(full(pre_tmp), full(pre_tmp)))
                    if part == 5:
                        steps.wait()
                        steps.did(tt(full(kk), full(kk), full(pre_tmp), ALU.mult))
                    if part == 6:
                        steps.wait()
                        sig(dve.scalar_tensor_tensor(out=full(a_c), in0=full(kk), scalar=-1.0, in1=full(e_before),
                                                     op0=ALU.mult, op1=ALU.mult), "chans")
                        steps.did(tt(full(k2), full(kk), full(rate), ALU.mult))
                    if part == 7:
                        steps.wait()
                        sig(tt(full(b_c), full(k2), full(e_inv), ALU.mult), "chans")
                    if part == 8:
                        sig(tt(full(bh_c), full(k2), full(e_rest), ALU.mult), "chans")
                    if part == 9:
                        wait("bonus_sum", 2, 1)
                        sig(tt(full(bonus), full(bank[2]), v_in(j), ALU.mult), "bonus_sum")

                def pair(j, last):
                    steps = Steps(dve, sem["dve_step"], j * RWKV_STEPS)
                    wait = lambda n, per=1, k=1: dve.wait_ge(sem[n], j * per + k)
                    col = lambda key: cols[key][:, bass.ds(j, 1)]
                    tt = lambda out, x, y_, op: dve.tensor_tensor(out, x, y_, op)
                    full = lambda x: x[:, :]
                    sig = lambda ins, n: ins.then_inc(sem[n], 1)
                    def masked(out, banks, mask, n, h):
                        sig(tt(quads(out[:, h, :]), quads(bank[banks[h]][:, :]), wide(mask, 4), ALU.mult), n)

                    for h in range(2):
                        wait("scores", 10, 1 + h)
                        masked(NT, (2, 3), upper[:, :], "masked", h)
                    for h in range(2):
                        wait("scores", 10, 3 + h)
                        masked(akT, (1, 4), upper[:, :], "masked", h)
                    wait("masked", 8, 2)
                    for h in range(2):
                        wait("scores", 10, 5 + h)
                        steps.did(tt(quads(Tm[:, h, :]), quads(bank[(5, 6)[h]][:, :]), wide(first[:, 0, :], 4), ALU.mult))
                        steps.did(tt(quads(Tt[:, h, :]), quads(NT[:, h, :]), wide(first[:, 1, :], 4), ALU.mult))
                        steps.wait()
                        for x in (Tm, Tt):
                            sig(tt(quads(x[:, h, :]), quads(x[:, h, :]), wide(ident[:, :], 4), ALU.add), "t_init")
                    for h in range(2):
                        wait("scores", 10, 7 + h)
                        masked(rbT, (7, 0), upper_incl[:, :], "masked", h)
                    for h in range(2):
                        wait("scores", 10, 9 + h)
                        masked(rkT, (2, 3), upper_incl[:, :], "masked", h)
                    wait("t_init", 4, 4)
                    for l in range(LEVELS):
                        for h in range(2):
                            wait("w_mm", 2 * LEVELS, 2 * l + h + 1)
                            masked(W, w_bank, level[:, l, :], "w_ev", h)
                        for h in range(2):
                            if l:
                                wait("t_ev", per_t, 4 * (l - 1) + 2 * h + 2)
                            wait("t_mm", 2 * LEVELS, 2 * l + h + 1)
                            sig(tt(Tt[:, h, :], Tt[:, h, :], full(bank[tt_bank[h]]), ALU.add), "t_ev")
                            if l < LEVELS - 1:
                                sig(tt(Tm[:, h, :], Tm[:, h, :], full(bank[tm_bank[h]]), ALU.add), "t_ev")
                        if not last:
                            prepare(j + 1, l if l < 4 else 9)
                    wait("mt_mm")
                    for par in range(2):
                        sig(tt(MT.rearrange("p (c two) k -> p two c k", two=2)[:, par], quads(bank[w_bank[par]][:, :]),
                               wide(block_ones[:, :], 4), ALU.mult), "mt_ev")
                    wait("q_mm")
                    wait("kept", 4, 8)
                    sig(tt(full(Q), full(r_k), full(bank[5]), ALU.add), "q_ev")
                    steps.did(dve.memset(S[:, 0, :], 0.0))
                    for c in range(NC - 1):
                        wait("f_mm", NC - 1, c + 1)
                        f = bank[f_bank[c % 2]][:, (c // 2) * P:(c // 2) * P + P]
                        if c == 0:
                            sig(dve.tensor_copy(S[:, 1, :], f), "state")
                        else:
                            wait("state", NC - 1, c)
                            sig(dve.scalar_tensor_tensor(
                                out=S[:, c + 1, :], in0=S[:, c, :], scalar=e_k[:, c * C + C - 1:c * C + C],
                                in1=f, op0=ALU.mult, op1=ALU.add), "state")
                        if not last and c < 5:
                            prepare(j + 1, 4 + c)
                    wait("state", NC - 1, NC - 1)
                    steps.wait()
                    sig(tt(S_own, S[:, :, :], wide(block_ones[:, :], NC), ALU.mult), "s_masked")
                    wait("mean_mm")
                    sig(dve.scalar_tensor_tensor(out=full(y), in0=full(bank[2]), scalar=-1.0 / C, in1=full(y),
                                                 op0=ALU.mult, op1=ALU.add), "centred")
                    wait("var_mm")
                    sig(dve.tensor_scalar(full(tmp), full(bank[3]), 1.0 / C, 64e-5, ALU.mult, ALU.add), "var")
                    wait("root")
                    steps.did(dve.reciprocal(full(tmp), full(tmp)))
                    steps.wait()
                    sig(tt(full(y), full(y), full(tmp), ALU.mult), "normed")
                    wait("affine")
                    steps.did(tt(full(y), full(y), full(bonus_k), ALU.add))
                    steps.wait()
                    sig(tt(mixed_T[:, bass.ds(CT + j, 1), :], full(y), full(gate_k), ALU.mult), "pair_done")
                    assert steps.n == RWKV_STEPS, steps.n

                for part in range(10):
                    prepare(0, part)
                with dve.Fori(0, CT - 1) as j:
                    pair(j, False)
                pair(CT - 1, True)
                dve.wait_ge(sem["pair_done"], CT + 1)


RWKV_STEPS = 7
PREPARE_STEPS = 7
PREPARED_BEFORE = (0, 0, 1, 3, 3, 5, 6, 7, 7, 7)


E = 32
EG = 8
NG = 4
FE = 512
KF = FE // P
OVER = 7
SLOTS = (E + OVER) * P
SKIP = 1 << 20
CHUNKS = 12
RING = 8


def project_out(nc, w, left_T, rows, KT, pairs, residual, ring, name, out=None):
    with Scope(nc, name) as s:
        g = Gemm(nc, s, ring, left_T, KT, pairs, lambda panel: w[:, bass.ds(panel * T, T)], channels=False)
        loaded, stored = s.sem("loaded"), s.sem("stored")
        with nc.Block() as block:
            @block.sync
            def _(sp):
                g.load_panel(sp, 0, 0, None)
                sp.dma_start(rows[:, :, :], residual.rearrange("(t p) d -> p t d", p=P)).then_inc(loaded, 16)
                g.load_panel(sp, 1, 1, None)
                with sp.Fori(0, pairs - 1) as i:
                    for slot in range(2):
                        g.load_panel(sp, 2 * i + 2 + slot, slot, i)
                if out is not None:
                    sp.wait_ge(g.bank_free, BANKS * (pairs + 1))
                    sp.dma_start(out.rearrange("(t p) d -> p t d", p=P), rows[:, :, :]).then_inc(stored, 16)
                    sp.wait_ge(stored, 16)

            block.tensor(g.tensor)

            @block.vector
            def _(dve):
                dve.wait_ge(loaded, 16)

                def add(bank, panel, sub, b, i):
                    cut = rows[:, sub, bass.ds(panel * T, T)]
                    dve.tensor_tensor(cut, cut, bank[:, :], ALU.add).then_inc(g.bank_free, 1)

                g.drain(dve, 0, pairs, add)
                dve.wait_ge(g.bank_free, BANKS * (pairs + 1))


def route(nc, a, v_T, ones, gates, table, over_expert, over_count, id_table, rows, normed):
    NL = NG + E
    with Scope(nc, "route") as s:
        w = s.sb("w", [P, KD, NL])
        bias = s.sb("bias", [1, NL])
        upper = s.sb("upper", [P, P])
        logits = s.sb("logits", [P, TT, NL])
        gpad, gtop, etop, esel = (s.sb(n, [P, TT, 8]) for n in ("gpad", "gtop", "etop", "esel"))
        gidx, eidx = s.sb("gidx", [P, TT, 8], U32), s.sb("eidx", [P, TT, 8], U32)
        lane = s.sb("lane", [P, E])
        hot_g, gexp = s.sb("hot_g", [P, TT, NG]), s.sb("gexp", [P, TT, NG])
        part = s.sb("part", [P, TT, EG])
        grp, gsum, pgrp, gap, egap, esum = (s.sb(n, [P, TT, 1]) for n in ("grp", "gsum", "pgrp", "gap", "egap", "esum"))
        eid = s.sb("eid", [P, TT, 2])
        hot = s.sb("hot", [P, 2, TT, E])
        both = s.sb("both", [P, TT, E])
        counts, blocks, more, upto = (s.sb(n, [P, E]) for n in ("counts", "blocks", "more", "upto"))
        moved, slot, far = s.sb("moved", [P, E]), s.sb("slot", [P, TT, E]), s.sb("far", [P, TT, E])
        dest, dest_i = s.sb("dest", [P, 2, TT]), s.sb("dest_i", [P, 2 * TT], I32)
        ids = s.sb("ids", [P, 2 * TT], I32)
        fill = s.sb("fill", [E + OVER, P], I32)
        block_no, before = s.sb("block_no", [1, OVER, E]), s.sb("before", [1, OVER])
        bank = s.banks(2)
        loaded, iotas, multiplied, step, exped, scattered, ranked, dest_ready, filled, read = (
            s.sem(n) for n in ("loaded", "iotas", "multiplied", "step", "exped", "scattered", "ranked", "dest_ready", "filled", "read"))
        hot_ready, gap_ready, centred, stored = s.sem("hot_ready"), s.sem("gap_ready"), s.sem("centred"), s.sem("stored")
        with nc.Block() as block:
            @block.sync
            def _(sp):
                sp.dma_start(w[:, :, 0:NG], a["router_group_w"][0].rearrange("(k p) g -> p k g", p=P)).then_inc(loaded, 16)
                sp.dma_start(w[:, :, NG:NL], a["router_expert_w"][0].rearrange("(k p) g -> p k g", p=P)).then_inc(loaded, 16)
                sp.dma_start(bias[:, 0:NG], a["router_group_b"]).then_inc(loaded, 16)
                sp.dma_start(bias[:, NG:NL], a["router_expert_b"]).then_inc(loaded, 16)
                sp.dma_start(normed.rearrange("(t p) d -> p t d", p=P), rows[:, :, :]).then_inc(stored, 16)
                sp.wait_ge(iotas, 1)
                sp.dma_start(id_table.rearrange("(b p) o -> b (p o)", p=P), fill[:, :]).then_inc(filled, 16)
                sp.wait_ge(scattered, 16 * 2 * TT)
                sp.dma_start(table[:, :], id_table.rearrange("(b p) o -> p (b o)", p=P),
                             allow_slow_non_contiguous=True).then_inc(read, 16)
                sp.wait_ge(read, 16)
                sp.wait_ge(stored, 16)

            @block.gpsimd
            def _(pool):
                pool.memset(fill[:, :], SKIP).then_inc(iotas, 1)
                pool.wait_ge(iotas, 1)
                pool.iota(lane[:, :], [[1, E]], base=0, channel_multiplier=0,
                          allow_small_or_imprecise_dtypes=True).then_inc(iotas, 1)
                pool.wait_ge(iotas, 2)
                pool.iota(ids[:, :], [[1, 2], [2 * P, TT]], base=0, channel_multiplier=2).then_inc(iotas, 1)
                pool.wait_ge(iotas, 3)
                pool.iota(block_no[:, :, :], [[1, OVER], [0, E]], base=0, channel_multiplier=0,
                          allow_small_or_imprecise_dtypes=True).then_inc(iotas, 1)
                pool.wait_ge(iotas, 4)
                pool.affine_select(out=upper[:, :], in_=ones[:, :], compare_op=ALU.is_gt, fill=0.0, base=0,
                                   pattern=[[1, P]], channel_multiplier=-1).then_inc(iotas, 1)
                pool.wait_ge(filled, 16)
                pool.wait_ge(dest_ready, 1)
                for i in range(2 * TT):
                    pool.indirect_dma_start(out=id_table, out_offset=bass.IndirectOffsetOnAxis(ap=dest_i[:, i:i + 1].bitcast(U32), axis=0),
                                            in_=ids[:, i:i + 1], in_offset=None).then_inc(scattered, 16)
                pool.wait_ge(scattered, 16 * 2 * TT)

            @block.tensor
            def _(pe):
                pe.wait_ge(loaded, 64)
                for t in range(TT):
                    out = bank[0][:, t * 64:t * 64 + NL]
                    for k in range(KD):
                        pe.matmul(out, v_T[:, k, t * P:(t + 1) * P], w[:, k, :], start=(k == 0), stop=False)
                    mm = pe.matmul(out, ones[0:1, :], bias[:, :], start=False, stop=True)
                mm.then_inc(multiplied, 1)
                pe.wait_ge(hot_ready, 1)
                pe.wait_ge(iotas, 5)
                for t in range(TT):
                    for u in range(t):
                        pe.matmul(bank[1][:, t * E:(t + 1) * E], ones[:, :], both[:, u, :], start=(u == 0), stop=False)
                    pe.matmul(bank[1][:, t * E:(t + 1) * E], upper[:, :], both[:, t, :], start=(t == 0), stop=True)
                for u in range(TT):
                    mm = pe.matmul(bank[1][:, TT * E:(TT + 1) * E], ones[:, :], both[:, u, :], start=(u == 0), stop=(u == TT - 1))
                mm.then_inc(ranked, 1)

            @block.scalar
            def _(act):
                act.wait_ge(centred, 1)
                act.activation(gexp[:, :, :], gexp[:, :, :], ACT.Exp).then_inc(exped, 1)
                act.wait_ge(gap_ready, 1)
                act.activation(egap[:, :, :], gap[:, :, :], ACT.Exp).then_inc(exped, 1)

            @block.vector
            def _(dve):
                steps = Steps(dve, step)

                def do(instruction):
                    steps.did(instruction)
                    steps.wait()

                tt, ts = dve.tensor_tensor, dve.tensor_scalar
                wide = lambda x, n: x.broadcast_to([P, TT, n])
                do(dve.memset(gpad[:, :, :], -3e38))
                dve.wait_ge(multiplied, 1)
                do(dve.tensor_copy(logits[:, :, :], bank[0][:, 0:TT * 64].rearrange("p (t n) -> p t n", n=64)[:, :, 0:NL]))
                do(dve.tensor_copy(gpad[:, :, 0:NG], logits[:, :, 0:NG]))
                for t in range(TT):
                    do(dve.max(gtop[:, t, :], gpad[:, t, :]))
                    do(dve.max_index(gidx[:, t, :], gtop[:, t, :], gpad[:, t, :]))
                tt(gexp[:, :, :], logits[:, :, 0:NG], wide(gtop[:, :, 0:1], NG), ALU.subtract).then_inc(centred, 1)
                do(dve.tensor_copy(grp[:, :, :], gidx[:, :, 0:1]))
                dve.wait_ge(iotas, 5)
                do(tt(hot_g[:, :, :], lane[:, 0:NG].unsqueeze(1).broadcast_to([P, TT, NG]), wide(grp[:, :, :], NG), ALU.is_equal))
                for g in range(NG):
                    out = esel if g == 0 else part
                    do(tt(out[:, :, :], logits[:, :, NG + g * EG:NG + (g + 1) * EG], wide(hot_g[:, :, g:g + 1], EG), ALU.mult))
                    if g:
                        do(tt(esel[:, :, :], esel[:, :, :], part[:, :, :], ALU.add))
                for t in range(TT):
                    do(dve.max(etop[:, t, :], esel[:, t, :]))
                    do(dve.max_index(eidx[:, t, :], etop[:, t, :], esel[:, t, :]))
                tt(gap[:, :, :], etop[:, :, 1:2], etop[:, :, 0:1], ALU.subtract).then_inc(gap_ready, 1)
                do(dve.tensor_copy(eid[:, :, :], eidx[:, :, 0:2]))
                do(ts(grp[:, :, :], grp[:, :, :], float(EG), None, ALU.mult))
                do(tt(eid[:, :, :], eid[:, :, :], wide(grp[:, :, :], 2), ALU.add))
                for c in range(2):
                    do(tt(hot[:, c, :, :], lane[:, :].unsqueeze(1).broadcast_to([P, TT, E]), wide(eid[:, :, c:c + 1], E), ALU.is_equal))
                tt(both[:, :, :], hot[:, 0, :, :], hot[:, 1, :, :], ALU.add).then_inc(hot_ready, 1)
                dve.wait_ge(exped, 1)
                do(dve.tensor_reduce(gsum[:, :, :], gexp[:, :, :], AX.X, ALU.add))
                do(dve.reciprocal(pgrp[:, :, :], gsum[:, :, :]))
                dve.wait_ge(exped, 2)
                do(ts(esum[:, :, :], egap[:, :, :], 1.0, None, ALU.add))
                do(dve.reciprocal(esum[:, :, :], esum[:, :, :]))
                do(tt(gates[:, :, 0:1], pgrp[:, :, :], esum[:, :, :], ALU.mult))
                do(tt(gates[:, :, 1:2], gates[:, :, 0:1], egap[:, :, :], ALU.mult))
                dve.wait_ge(ranked, 1)
                do(dve.tensor_copy(counts[:, :], bank[1][:, TT * E:(TT + 1) * E]))
                do(ts(blocks[:, :], counts[:, :], float(P), None, ALU.is_gt))
                for n in (2 * P, 3 * P):
                    do(ts(more[:, :], counts[:, :], float(n), None, ALU.is_gt))
                    do(tt(blocks[:, :], blocks[:, :], more[:, :], ALU.add))
                do(dve.tensor_tensor_scan(upto[:, :], ones[:, 0:E], blocks[:, :], 0.0, ALU.mult, ALU.add))
                do(tt(moved[:, :], upto[:, :], blocks[:, :], ALU.subtract))
                do(tt(moved[:, :], moved[:, :], lane[:, :], ALU.subtract))
                do(ts(moved[:, :], moved[:, :], float(P), float((E - 1) * P), ALU.mult, ALU.add))
                rank = bank[1][:, 0:TT * E].rearrange("p (t e) -> p t e", e=E)
                do(ts(far[:, :, :], rank, float(P), None, ALU.is_ge))
                do(tt(far[:, :, :], far[:, :, :], moved[:, :].unsqueeze(1).broadcast_to([P, TT, E]), ALU.mult))
                do(tt(slot[:, :, :], rank, far[:, :, :], ALU.add))
                do(ts(more[:, :], lane[:, :], float(P), None, ALU.mult))
                do(tt(slot[:, :, :], slot[:, :, :], more[:, :].unsqueeze(1).broadcast_to([P, TT, E]), ALU.add))
                for c in range(2):
                    do(tt(far[:, :, :], slot[:, :, :], hot[:, c, :, :], ALU.mult))
                    do(dve.tensor_reduce(dest[:, c, :], far[:, :, :], AX.X, ALU.add))
                dve.tensor_copy(dest_i[:, :], dest[:, :, :].rearrange("p c t -> p (c t)")).then_inc(dest_ready, 1)
                do(tt(block_no[:, :, :], upto[0:1, :].unsqueeze(1).broadcast_to([1, OVER, E]), block_no[:, :, :], ALU.is_le))
                do(dve.tensor_reduce(before[:, :], block_no[:, :, :], AX.X, ALU.add))
                do(ts(before[:, :], before[:, :], float(E - 1), None, ALU.min))
                do(dve.tensor_copy(over_expert[:, :], before[:, :]))
                do(dve.tensor_copy(over_count[:, :], upto[0:1, E - 1:E]))


class Expert:

    def __init__(self, nc, s, a_in, gain, ident, normed, results, table, takes, doubled):
        self.a_in, self.gain, self.ident, self.normed, self.results = a_in, gain, ident, normed, results
        self.table, self.takes, self.doubled = table, takes, doubled
        self.ring = [s.sb(f"ring{i}", [P, 4, T]) for i in range(RING)]
        self.x = [s.sb(f"x{i}", [P, D]) for i in range(doubled)]
        self.x_T = [s.sb(f"x_T{i}", [P, KD, P]) for i in range(doubled)]
        self.y = [s.sb(f"y{i}", [P, D]) for i in range(doubled)]
        self.take = [s.sb(f"take{i}", [P, 1], I32) for i in range(doubled)]
        self.put = [s.sb(f"put{i}", [P, 1], I32) for i in range(doubled)]
        self.silu, self.hidden, self.hidden_T = (s.sb(n, [P, T]) for n in ("silu", "hidden", "hidden_T"))
        self.gate_bank, self.up_bank, b2, b3, self.hid_bank, _, b6, b7 = s.banks()
        self.x_bank, self.y_bank = (b2, b3), (b6, b7)
        self.arrived = [s.sem(f"arrived{i}") for i in range(RING)]
        self.used = [s.sem(f"used{i}") for i in range(RING)]
        self.gathered = [s.sem(f"gathered{i}") for i in range(doubled)]
        self.scattered = [s.sem(f"scattered{i}") for i in range(doubled)]
        self.turned, self.x_ready, self.silu_ready, self.hidden_ready, self.hid_turned, self.hid_copied = (
            s.sem(n) for n in ("turned", "x_ready", "silu_ready", "hidden_ready", "hid_turned", "hid_copied"))
        self.y_ready, self.take_ready, self.put_ready, self.cleared, self.passed = (
            s.sem(n) for n in ("y_ready", "take_ready", "put_ready", "cleared", "passed"))

    def bounds(self, pool):
        self.last_row, self.last_result = pool.to_reg(T - 1), pool.to_reg(2 * T - 1)

    def load(self, sp, e, chunk, slot, wait_uses):
        if wait_uses is not None:
            sp.wait_ge(self.used[slot], wait_uses)
        which, q = divmod(chunk, 4)
        if which == 2:
            view = self.a_in["expert_w_down"][0, e, :, q * T:(q + 1) * T]
        else:
            view = self.a_in["expert_w_gate" if which == 0 else "expert_w_up"][0, e, q * T:(q + 1) * T, :]
        sp.dma_start(self.ring[slot][:, :, :], view.rearrange("(k p) c -> p k c", p=P)).then_inc(self.arrived[slot], 16)

    def gather(self, pool, column, a, n):
        pool.tensor_copy(self.take[a][:, :], self.takes[:, column]).then_inc(self.take_ready, 1)
        pool.wait_ge(self.take_ready, n + 1)
        pool.sem_inc(self.passed, 1)
        pool.indirect_dma_start(out=self.x[a][:, :], out_offset=None, in_=self.normed,
                                in_offset=bass.IndirectOffsetOnAxis(ap=self.take[a][:, :].bitcast(U32), axis=0),
                                bounds_check=self.last_row, oob_is_err=False).then_inc(self.gathered[a], 16)

    def scatter(self, pool, column, a, n):
        pool.tensor_copy(self.put[a][:, :], self.table[:, column]).then_inc(self.put_ready, 1)
        pool.wait_ge(self.put_ready, n + 1)
        pool.wait_ge(self.y_ready, 4 * n + 4)
        pool.sem_inc(self.passed, 1)
        pool.indirect_dma_start(out=self.results,
                                out_offset=bass.IndirectOffsetOnAxis(ap=self.put[a][:, :].bitcast(U32), axis=0),
                                in_=self.y[a][:, :], in_offset=None,
                                bounds_check=self.last_result, oob_is_err=False).then_inc(self.scattered[a], 16)

    def turn(self, pe, a, n, turn):
        pe.wait_ge(self.gathered[a], 16 * turn + 16)
        for g in range(4):
            if g >= 2:
                pe.wait_ge(self.x_ready, 4 * n + g - 1)
            for k in range(4):
                mm = pe.transpose(self.x_bank[g % 2][:, k * P:(k + 1) * P],
                                  self.x[a][:, (4 * g + k) * P:(4 * g + k + 1) * P], self.ident[:, :])
            mm.then_inc(self.turned, 1)

    def products(self, pe, a, n, place, between=None):
        pe.wait_ge(self.x_ready, 4 * n + 4)
        for chunk in range(CHUNKS):
            if chunk == 8:
                if between is not None:
                    between()
                pe.wait_ge(self.hidden_ready, n + 1)
                for f in range(KF):
                    mm = pe.transpose(self.hid_bank[:, f * P:(f + 1) * P], self.hidden[:, f * P:(f + 1) * P], self.ident[:, :])
                mm.then_inc(self.hid_turned, 1)
                pe.wait_ge(self.hid_copied, n + 1)
            slot, uses = place(chunk)
            which, q = divmod(chunk, 4)
            pe.wait_ge(self.arrived[slot], 16 * uses + 16)
            if which == 2 and q >= 2:
                pe.wait_ge(self.y_ready, 4 * n + q - 1)
            for k in range(4):
                if which == 2:
                    mm = pe.matmul(self.y_bank[q % 2][:, :], self.hidden_T[:, k * P:(k + 1) * P], self.ring[slot][:, k, :],
                                   start=(k == 0), stop=(k == 3))
                else:
                    mm = pe.matmul((self.gate_bank, self.up_bank)[which][:, :], self.x_T[a][:, 4 * q + k, :],
                                   self.ring[slot][:, k, :], start=(q == 0 and k == 0), stop=(q == 3 and k == 3))
            mm.then_inc(self.used[slot], 1)

    def activate(self, act, a, n, turn, place):
        slot, uses = place(3)
        act.wait_ge(self.used[slot], uses + 1)
        act.activation(self.silu[:, :], self.gate_bank[:, :], ACT.Silu).then_inc(self.silu_ready, 1)
        act.wait_ge(self.hid_turned, n + 1)
        act.activation(self.hidden_T[:, :], self.hid_bank[:, :], ACT.Copy).then_inc(self.hid_copied, 1)
        if turn is not None:
            act.wait_ge(self.scattered[a], 16 * turn)
        for q in range(4):
            slot, uses = place(8 + q)
            act.wait_ge(self.used[slot], uses + 1)
            act.activation(self.y[a][:, q * T:(q + 1) * T], self.y_bank[q % 2][:, :], ACT.Copy).then_inc(self.y_ready, 1)

    def take_x(self, dve, a, n):
        for g in range(4):
            dve.wait_ge(self.turned, 4 * n + g + 1)
            gain = self.gain[:, 4 * g:4 * g + 4].unsqueeze(2).broadcast_to([P, 4, P])
            dve.tensor_tensor(self.x_T[a][:, 4 * g:4 * g + 4, :], self.x_bank[g % 2][:, :].rearrange("p (k s) -> p k s", s=P),
                              gain, ALU.mult).then_inc(self.x_ready, 1)

    def hide(self, dve, n, place):
        slot, uses = place(7)
        dve.wait_ge(self.used[slot], uses + 1)
        dve.wait_ge(self.silu_ready, n + 1)
        dve.tensor_tensor(self.hidden[:, :], self.silu[:, :], self.up_bank[:, :], ALU.mult).then_inc(self.hidden_ready, 1)


def experts(nc, a, gain, ident, normed, results, table, takes):
    with Scope(nc, "experts") as s:
        x = Expert(nc, s, a, gain, ident, normed, results, table, takes, 2)
        turns = E // 2

        def place(i, b):
            return lambda chunk: ((b * CHUNKS + chunk) % RING, 3 * i + (b * CHUNKS + chunk) // RING)

        with nc.Block() as block:
            @block.sync
            def _(sp):
                def load(i, c, wait=True):
                    x.load(sp, 2 * i + c // CHUNKS, c % CHUNKS, c % RING, 3 * i + c // RING if wait else None)

                for c in range(RING):
                    load(0, c, wait=False)
                with sp.Fori(0, turns - 1) as i:
                    for c in range(RING, 2 * CHUNKS + RING):
                        load(i, c)
                for c in range(RING, 2 * CHUNKS):
                    load(turns - 1, c)

            @block.gpsimd
            def _(pool):
                x.bounds(pool)
                pool.wait_ge(x.cleared, 2)
                x.gather(pool, slice(0, 1), 0, 0)

                def turn(i, last):
                    for b in range(2):
                        n = 2 * i + b
                        if not (last and b):
                            pool.wait_ge(x.turned, 4 * n + 1)
                            x.gather(pool, bass.ds(n + 1, 1), 1 - b, n + 1)
                        x.scatter(pool, bass.ds(n, 1), b, n)

                with pool.Fori(0, turns - 1) as i:
                    turn(i, False)
                turn(turns - 1, True)
                for b in range(2):
                    pool.wait_ge(x.scattered[b], 16 * turns)

            @block.tensor
            def _(pe):
                def turn(i, last):
                    x.products(pe, 0, 2 * i, place(i, 0), lambda: x.turn(pe, 1, 2 * i + 1, i))
                    x.products(pe, 1, 2 * i + 1, place(i, 1), None if last else lambda: x.turn(pe, 0, 2 * i + 2, i + 1))

                x.turn(pe, 0, 0, 0)
                with pe.Fori(0, turns - 1) as i:
                    turn(i, False)
                turn(turns - 1, True)

            @block.scalar
            def _(act):
                for b in range(2):
                    x.activate(act, b, b, None, place(0, b))
                with act.Fori(1, turns) as i:
                    for b in range(2):
                        x.activate(act, b, 2 * i + b, i, place(i, b))

            @block.vector
            def _(dve):
                for b in range(2):
                    dve.memset(x.x[b][:, :], 0.0).then_inc(x.cleared, 1)
                x.take_x(dve, 0, 0)

                def turn(i, last):
                    for b in range(2):
                        x.hide(dve, 2 * i + b, place(i, b))
                        if not (last and b):
                            x.take_x(dve, 1 - b, 2 * i + b + 1)

                with dve.Fori(0, turns - 1) as i:
                    turn(i, False)
                turn(turns - 1, True)


def overflow(nc, a, gain, ident, normed, results, table, takes, over_expert, over_count):
    with Scope(nc, "overflow") as s:
        x = Expert(nc, s, a, gain, ident, normed, results, table, takes, 1)
        free = s.sem("free")

        def place(b):
            return lambda chunk: (chunk % RING, b * (2 if chunk % RING < CHUNKS - RING else 1) + chunk // RING)

        def each(eng, part):
            count = eng.value_load(over_count[0:1, 0:1], min_val=0, max_val=OVER)
            with eng.If(count > 0):
                with eng.Fori(0, count) as b:
                    part(b)

        with nc.Block() as block:
            @block.sync
            def _(sp):
                def part(b):
                    e = sp.value_load(over_expert[0:1, bass.ds(b, 1)], min_val=0, max_val=E - 1)
                    sp.wait_ge(free, b + 1)
                    for chunk in range(CHUNKS):
                        slot, uses = place(b)(chunk)
                        x.load(sp, e, chunk, slot, uses if chunk >= RING else None)
                each(sp, part)

            @block.gpsimd
            def _(pool):
                x.bounds(pool)
                pool.sem_inc(free, 1)
                pool.wait_ge(x.cleared, 1)

                def part(b):
                    x.gather(pool, bass.ds(E + b, 1), 0, b)
                    x.scatter(pool, bass.ds(E + b, 1), 0, b)
                    pool.wait_ge(x.scattered[0], 16 * b + 16)
                    pool.sem_inc(free, 1)
                each(pool, part)

            @block.tensor
            def _(pe):
                def part(b):
                    x.turn(pe, 0, b, b)
                    x.products(pe, 0, b, place(b))
                each(pe, part)

            @block.scalar
            def _(act):
                each(act, lambda b: x.activate(act, 0, b, None, place(b)))

            @block.vector
            def _(dve):
                dve.memset(x.x[0][:, :], 0.0).then_inc(x.cleared, 1)

                def part(b):
                    x.take_x(dve, 0, b)
                    x.hide(dve, b, place(b))
                each(dve, part)


def linear(nc, name, ring, left_T, KT, pairs, weights, put, odd=False):
    with Scope(nc, name) as s:
        g = Gemm(nc, s, ring, left_T, KT, pairs, weights, True, odd)
        with nc.Block() as block:
            block.sync(g.sync)
            block.tensor(g.tensor)

            @block.scalar
            def _(act):
                def copy(bank, panel, sub, b, i):
                    put(act, bank, panel, sub).then_inc(g.bank_free, 1)

                if pairs:
                    g.drain(act, 0, pairs, copy)
                if odd:
                    g.drain_turn(act, pairs, (0,), copy)
                act.wait_ge(g.bank_free, BANKS * (pairs + 1) + (4 if odd else 0))


def gated(nc, name, ring, left_T, KT, pairs, weights, gate, combine):
    with Scope(nc, name) as s:
        g = Gemm(nc, s, ring, left_T, KT, pairs, weights, True)
        stage = s.sb("stage", [P, BANKS, T])
        staged, taken, partial = s.sem("staged"), s.sem("taken"), s.sem("partial")
        with nc.Block() as block:
            block.sync(g.sync)
            block.tensor(g.tensor)

            @block.scalar
            def _(act):
                act.sem_inc(taken, BANKS)

                def copy(bank, panel, sub, b, i):
                    act.wait_ge(taken, BANKS * i + b + 1)
                    gate(act, stage[:, b, :], bank, panel, sub).then_inc(g.bank_free, 1)

                g.drain(act, 0, pairs, copy)

            @block.vector
            def _(dve):
                with dve.Fori(0, pairs) as i:
                    n = 0
                    for slot in range(2):
                        for sub in range(4):
                            b = 4 * slot + sub
                            dve.wait_ge(g.bank_free, BANKS * i + b + 1 + BANKS)
                            parts = combine(dve, stage[:, b, :], 2 * i + slot, sub)
                            for part in parts[:-1]:
                                part().then_inc(partial, 1)
                                n += 1
                                dve.wait_ge(partial, BANKS * (len(parts) - 1) * i + n)
                            parts[-1]().then_inc(taken, 1)
                dve.wait_ge(taken, BANKS * (pairs + 1))


def finish_block_one(nc, results, gates, residual, gain, rows, out):
    with Scope(nc, "finish_one") as s:
        y = s.sb("y", [P, TT, 2, D])
        gain_row = s.sb("gain_row", [P, D])
        square = s.sb("square", [P, D])
        stat, root, inv = s.sb("stat", [P, TT]), s.sb("root", [P, TT]), s.sb("inv", [P, TT])
        loaded = [s.sem(f"loaded{t}") for t in range(TT)]
        gain_loaded, added, squared, averaged, rooted, inverted, scaled, stored = (
            s.sem(n) for n in ("gain_loaded", "added", "squared", "averaged", "rooted", "inverted", "scaled", "stored"))
        with nc.Block() as block:
            @block.sync
            def _(sp):
                tiles = lambda x: x.rearrange("(t p) d -> p t d", p=P)
                for t in range(TT):
                    sp.dma_start(rows[:, t, :], tiles(residual)[:, t, :]).then_inc(loaded[t], 16)
                    sp.dma_start(y[:, t, :, :], results.rearrange("(t p c) d -> p t c d", p=P, c=2)[:, t]).then_inc(loaded[t], 16)
                sp.dma_start(gain_row[:, :], gain.unsqueeze(0).broadcast_to([P, D])).then_inc(gain_loaded, 16)
                for t in range(TT):
                    sp.wait_ge(scaled, t + 1)
                    sp.dma_start(tiles(out)[:, t, :], rows[:, t, :]).then_inc(stored, 16)
                sp.wait_ge(stored, 16 * TT)

            @block.vector
            def _(dve):
                def scale(t):
                    dve.wait_ge(rooted, t + 1)
                    dve.reciprocal(inv[:, t:t + 1], root[:, t:t + 1]).then_inc(inverted, 1)
                    dve.wait_ge(inverted, t + 1)
                    if t == 0:
                        dve.wait_ge(gain_loaded, 16)
                    dve.scalar_tensor_tensor(out=rows[:, t, :], in0=rows[:, t, :], scalar=inv[:, t:t + 1], in1=gain_row[:, :],
                                             op0=ALU.mult, op1=ALU.mult).then_inc(scaled, 1)

                for t in range(TT):
                    dve.wait_ge(loaded[t], 32)
                    for c in range(2):
                        if c:
                            dve.wait_ge(added, 2 * t + 1)
                        dve.scalar_tensor_tensor(out=rows[:, t, :], in0=y[:, t, c, :], scalar=gates[:, t, c:c + 1],
                                                 in1=rows[:, t, :], op0=ALU.mult, op1=ALU.add).then_inc(added, 1)
                    dve.wait_ge(squared, t + 1)
                    dve.tensor_scalar(root[:, t:t + 1], stat[:, t:t + 1], 1.0 / D, 1e-6, ALU.mult, ALU.add).then_inc(averaged, 1)
                for t in range(TT):
                    scale(t)

            @block.scalar
            def _(act):
                for t in range(TT):
                    act.wait_ge(added, 2 * t + 2)
                    if t:
                        act.wait_ge(squared, t)
                    act.activation(square[:, :], rows[:, t, :], ACT.Square, accum_out=stat[:, t:t + 1]).then_inc(squared, 1)
                act.wait_ge(averaged, TT)
                for t in range(TT):
                    act.activation(root[:, t:t + 1], root[:, t:t + 1], ACT.Sqrt).then_inc(rooted, 1)


QH, KVH, HD = 16, 4, 64
QT, KTL = 8, 8
VTL, GTL = 10, 12


def attention(nc, att_T, ident, block_ones, q_gain, k_gain, sinks, ones):
    scale = 1.0 / math.sqrt(HD)
    with Scope(nc, "attention") as s:
        swap = s.sb("swap", [P, P])
        k_swap = s.sb("k_swap", [P, 2, T])
        v_t = s.sb("v_t", [P, TT, KVH * HD])
        square = s.sb("square", [P, 10, T])
        inv = s.sb("inv", [P, 2, T])
        masks = s.sb("masks", [P, 2, 2 * P])
        sink = s.sb("sink", [P, QH])
        sink_row = s.sb("sink_row", [1, QH])
        bank = s.banks()
        names = ["made", "made2", "loaded", "squared", "summed", "var", "root", "inverted", "normed", "swapped", "swap_copied",
                 "v_turned", "v_copied", "sunk", "sink_copied", "silu"]
        sem = {n: s.sem(n) for n in names}
        with nc.Block() as block:
            @block.sync
            def _(sp):
                sp.dma_start(sink_row[:, :], sinks.unsqueeze(0)).then_inc(sem["loaded"], 16)

            @block.gpsimd
            def _(pool):
                pool.memset(masks[:, :, :], 0.0).then_inc(sem["made"], 1)
                pool.wait_ge(sem["made"], 1)
                pool.affine_select(out=masks[:, :, :], in_=masks[:, :, :], compare_op=ALU.is_gt, fill=-8e30, base=0,
                                   pattern=[[0, 2], [1, 2 * P]], channel_multiplier=-1).then_inc(sem["made"], 1)
                pool.wait_ge(sem["made"], 2)
                pool.affine_select(out=masks[:, :, :], in_=masks[:, :, :], compare_op=ALU.is_ge, fill=-8e30, base=P,
                                   pattern=[[0, 2], [-1, 2 * P]], channel_multiplier=1).then_inc(sem["made"], 1)
                pool.wait_ge(sem["made"], 3)
                pool.memset(masks[:, 0, 0:P], -8e30).then_inc(sem["made"], 1)
                pool.wait_ge(sem["made"], 4)

            @block.scalar
            def _(act):
                for t in range(10):
                    act.activation(square[:, t, :], att_T[:, t, :], ACT.Square).then_inc(sem["squared"], 1)
                for t in range(10):
                    act.wait_ge(sem["var"], t + 1)
                    act.activation(square[:, t, :], square[:, t, :], ACT.Sqrt).then_inc(sem["root"], 1)
                for t in range(8):
                    act.activation(att_T[:, GTL + t, :], att_T[:, GTL + t, :], ACT.Silu).then_inc(sem["silu"], 1)
                act.wait_ge(sem["silu"], 8)

            @block.tensor
            def _(pe):
                for t in range(10):
                    pe.wait_ge(sem["squared"], t + 1)
                    if t >= 2:
                        pe.wait_ge(sem["var"], t - 1)
                    pe.matmul(bank[t % 2][:, :], block_ones[:, :], square[:, t, :], start=True, stop=True).then_inc(sem["summed"], 1)
                for t in range(2):
                    for i in range(TT):
                        mm = pe.transpose(bank[2 + t][:, i * P:(i + 1) * P], att_T[:, VTL + t, i * P:(i + 1) * P], ident[:, :])
                mm.then_inc(sem["v_turned"], 1)
                pe.wait_ge(sem["loaded"], 16)
                pe.matmul(bank[4][:, 0:QH], ones[0:1, :], sink_row[:, :], start=True, stop=True).then_inc(sem["sunk"], 1)
                pe.wait_ge(sem["normed"], 10)
                pe.wait_ge(sem["made2"], 2)
                for t in range(2):
                    mm = pe.matmul(bank[5 + t][:, :], swap[:, :], att_T[:, KTL + t, :], start=True, stop=True)
                mm.then_inc(sem["swapped"], 1)

            @block.vector
            def _(dve):
                dve.tensor_copy(swap[:, 0:HD], ident[:, HD:P]).then_inc(sem["made2"], 1)
                dve.tensor_copy(swap[:, HD:P], ident[:, 0:HD]).then_inc(sem["made2"], 1)
                for t in range(10):
                    dve.wait_ge(sem["summed"], t + 1)
                    dve.tensor_scalar(square[:, t, :], bank[t % 2][:, :], 1.0 / HD, 1e-6, ALU.mult, ALU.add).then_inc(sem["var"], 1)
                dve.wait_ge(sem["v_turned"], 1)
                for t in range(2):
                    dve.tensor_copy(v_t[:, :, t * P:(t + 1) * P], bank[2 + t][:, :].rearrange("p (i c) -> p i c", c=P)).then_inc(sem["v_copied"], 1)
                dve.wait_ge(sem["sunk"], 1)
                dve.tensor_copy(sink[:, :], bank[4][:, 0:QH]).then_inc(sem["sink_copied"], 1)
                for t in range(10):
                    dve.wait_ge(sem["root"], t + 1)
                    if t >= 2:
                        dve.wait_ge(sem["normed"], t - 1)
                    dve.reciprocal(inv[:, t % 2, :], square[:, t, :]).then_inc(sem["inverted"], 1)
                    dve.wait_ge(sem["inverted"], t + 1)
                    dve.scalar_tensor_tensor(out=att_T[:, t, :], in0=att_T[:, t, :], scalar=(q_gain if t < 8 else k_gain),
                                             in1=inv[:, t % 2, :], op0=ALU.mult, op1=ALU.mult).then_inc(sem["normed"], 1)
                dve.wait_ge(sem["swapped"], 1)
                for t in range(2):
                    dve.tensor_copy(k_swap[:, t, :], bank[5 + t][:, :]).then_inc(sem["swap_copied"], 1)
                dve.wait_ge(sem["swap_copied"], 2)

        scores = s.sb("scores", [P, 2, 4, 2 * P])
        probs = s.sb("probs", [P, 2, 4, 2 * P])
        probs_T = s.sb("probs_T", [P, 2, 4, 2 * P])
        top, neg, total, sink_e, inv_e = (s.sb(n, [P, 2, 4]) for n in ("top", "neg", "total", "sink_e", "inv_e"))
        names = ["scored", "masked", "peak", "negated", "exped", "sink_in", "sink_exped", "dve_step", "normal", "turned",
                 "copied", "summed_up", "put"]
        sem = {n: s.sem("s_" + n) for n in names}
        steps = [(g, n) for g in range(KVH) for n in range(TT)]
        head = lambda g, par, pair: 4 * g + 2 * pair + par

        def key(g, par, cut):
            src = att_T[:, KTL + g // 2, :] if g % 2 == par else k_swap[:, g // 2, :]
            return src[par * HD:(par + 1) * HD, cut]

        with nc.Block() as block:
            @block.tensor
            def _(pe):
                def score(i):
                    g, n = steps[i]
                    if i >= 2:
                        pe.wait_ge(sem["masked"], 2 * (i - 1))
                    for par in range(2):
                        for pair in range(2):
                            h = head(g, par, pair)
                            for half in range(2):
                                blk = max(n - 1 + half, 0)
                                mm = pe.matmul(bank[(i % 2) * 2 + par][:, (2 * pair + half) * P:(2 * pair + half + 1) * P],
                                               att_T[par * HD:(par + 1) * HD, h // 2, n * P:(n + 1) * P],
                                               key(g, par, slice(blk * P, blk * P + P)), start=True, stop=True)
                        mm.then_inc(sem["scored"], 1)

                score(0)
                for i, (g, n) in enumerate(steps):
                    if i + 1 < len(steps):
                        score(i + 1)
                    pe.wait_ge(sem["normal"], 4 * (i + 1))
                    for par in range(2):
                        if i:
                            pe.wait_ge(sem["copied"], 2 * (i - 1) + par + 1)
                        for pair in range(2):
                            for half in range(2):
                                c = (2 * pair + half) * P
                                mm = pe.transpose(bank[4 + par][:, c:c + P],
                                                  probs[:, i % 2, 2 * par + pair, half * P:(half + 1) * P], ident[:, :])
                        mm.then_inc(sem["turned"], 1)
                    if i >= 2:
                        pe.wait_ge(sem["put"], i - 1)
                    for par in range(2):
                        pe.wait_ge(sem["copied"], 2 * i + par + 1)
                        for pair in range(2):
                            for half in range(2):
                                blk = max(n - 1 + half, 0)
                                mm = pe.matmul(bank[6 + i % 2][par * HD:(par + 1) * HD, pair * P:(pair + 1) * P],
                                               v_t[:, blk, g * HD:(g + 1) * HD],
                                               probs_T[:, i % 2, 2 * par + pair, half * P:(half + 1) * P],
                                               start=(half == 0), stop=(half == 1))
                    mm.then_inc(sem["summed_up"], 1)

            @block.vector
            def _(dve):
                def soften(i):
                    g, n = steps[i]
                    at = i % 2
                    if i >= 2:
                        dve.wait_ge(sem["exped"], 4 * (i - 1))
                    for par in range(2):
                        dve.wait_ge(sem["scored"], 2 * i + par + 1)
                        dve.tensor_tensor(scores[:, at, 2 * par:2 * par + 2, :],
                                          bank[(i % 2) * 2 + par][:, :].rearrange("p (a k) -> p a k", a=2),
                                          masks[:, min(n, 1), :].unsqueeze(1).broadcast_to([P, 2, 2 * P]),
                                          ALU.add).then_inc(sem["masked"], 1)
                    dve.wait_ge(sem["masked"], 2 * i + 2)
                    dve.tensor_reduce(top[:, at, :], scores[:, at, :, :], AX.X, ALU.max).then_inc(sem["peak"], 1)
                    dve.wait_ge(sem["peak"], i + 1)
                    own = sink[:, 4 * g:4 * g + 4].rearrange("p (pair par) -> p par pair", par=2)
                    two = lambda x: x[:, at, :].rearrange("p (par pair) -> p par pair", par=2)
                    dve.scalar_tensor_tensor(out=two(top), in0=two(top), scalar=scale, in1=own, op0=ALU.mult,
                                             op1=ALU.max).then_inc(sem["dve_step"], 1)
                    dve.wait_ge(sem["dve_step"], 3 * i + 1)
                    if i >= 2:
                        dve.wait_ge(sem["sink_exped"], i - 1)
                    dve.tensor_scalar(neg[:, at, :], top[:, at, :], -1.0, None, ALU.mult).then_inc(sem["negated"], 1)
                    dve.tensor_tensor(two(sink_e), own, two(top), ALU.subtract).then_inc(sem["sink_in"], 1)
                    dve.wait_ge(sem["exped"], 4 * i + 4)
                    dve.wait_ge(sem["sink_exped"], i + 1)
                    dve.tensor_tensor(total[:, at, :], total[:, at, :], sink_e[:, at, :], ALU.add).then_inc(sem["dve_step"], 1)
                    dve.wait_ge(sem["dve_step"], 3 * i + 2)
                    dve.reciprocal(inv_e[:, at, :], total[:, at, :]).then_inc(sem["dve_step"], 1)
                    dve.wait_ge(sem["dve_step"], 3 * i + 3)
                    for j in range(4):
                        dve.tensor_scalar(probs[:, at, j, :], probs[:, at, j, :], inv_e[:, at, j:j + 1], None,
                                          ALU.mult).then_inc(sem["normal"], 1)

                def put(i):
                    g, n = steps[i]
                    dve.wait_ge(sem["summed_up"], i + 1)
                    cut = slice(n * P, (n + 1) * P)
                    dve.tensor_tensor(att_T[:, 2 * g:2 * g + 2, cut], bank[6 + i % 2][:, 0:2 * P].rearrange("p (a q) -> p a q", a=2),
                                      att_T[:, GTL + 2 * g:GTL + 2 * g + 2, cut], ALU.mult).then_inc(sem["put"], 1)

                for i in range(len(steps)):
                    soften(i)
                    if i:
                        put(i - 1)
                put(len(steps) - 1)
                dve.wait_ge(sem["put"], len(steps))

            @block.scalar
            def _(act):
                for i in range(len(steps)):
                    at = i % 2
                    act.wait_ge(sem["negated"], i + 1)
                    if i >= 2:
                        act.wait_ge(sem["turned"], 2 * (i - 1))
                    for j in range(4):
                        act.activation(probs[:, at, j, :], scores[:, at, j, :], ACT.Exp, bias=neg[:, at, j:j + 1],
                                       scale=scale, accum_out=total[:, at, j:j + 1]).then_inc(sem["exped"], 1)
                    act.wait_ge(sem["sink_in"], i + 1)
                    act.activation(sink_e[:, at, :], sink_e[:, at, :], ACT.Exp).then_inc(sem["sink_exped"], 1)
                    for par in range(2):
                        act.wait_ge(sem["turned"], 2 * i + par + 1)
                        if i >= 2:
                            act.wait_ge(sem["summed_up"], i - 1)
                        act.activation(probs_T[:, at, 2 * par:2 * par + 2, :], bank[4 + par][:, :].rearrange("p (a k) -> p a k", a=2),
                                       ACT.Copy).then_inc(sem["copied"], 1)


SG, SC = 64, 16
SP_ = 64
CH = 8
NCH = T // CH
GB = 8
NB = SG // GB


def ssm(nc, a, u_dram, y_T, ident, ones):
    with Scope(nc, "ssm") as s:
        names = ["loaded", "turned", "copied", "step", "act_step", "pool_step"]
        sem = {n: s.sem(n) for n in names}
        B1, B2, Q1, Q2 = (s.sb(n, [P, SG * SC]) for n in ("B1", "B2", "Q1", "Q2"))
        fwd, fwd_s = s.sb("fwd", [P, SG, CH + 1]), s.sb("fwd_s", [P, SG, CH + 1])
        rev, rev_s = s.sb("rev", [P, SG, CH]), s.sb("rev_s", [P, SG, CH])
        sign = s.sb("sign", [P, 1])
        with Scope(nc, "ssm_tables") as s2:
            rows = s2.sb("rows", [SG, 2, P])
            dt_row = s2.sb("dt_row", [1, SG])
            c_rows = s2.sb("c_rows", [P, NB, 2, P])
            t = {n: s2.sb(n, [P, SG]) for n in ("are", "aim", "dt", "mag", "th", "k", "sn", "cs", "re", "im", "im_s", "den",
                                                 "cr", "ci", "ci_s", "x0", "x1", "mag_in")}
            bank = s2.banks(6)
            with nc.Block() as block:
                @block.sync
                def _(sp):
                    for half in range(2):
                        cut = slice(half * SP_, (half + 1) * SP_)
                        sp.dma_start(rows[:, 0, cut], a["A_re_2"]).then_inc(sem["loaded"], 16)
                        sp.dma_start(rows[:, 1, cut], a["A_im_2"]).then_inc(sem["loaded"], 16)
                    sp.dma_start(dt_row[:, :], a["log_dt_2"].unsqueeze(0)).then_inc(sem["loaded"], 16)
                    for order in range(2):
                        for part in range(2):
                            c = a[("C_re_2", "C_im_2")[part ^ order]].rearrange("(b g) h p -> (g h) b p", g=GB)
                            sp.dma_start(c_rows[:, :, order, part * SP_:(part + 1) * SP_], c).then_inc(sem["loaded"], 16)
                    for out, order in ((B1, 0), (B2, 1)):
                        for part in range(2):
                            b = a[("B_re_2", "B_im_2")[part ^ order]].rearrange("g p h -> p g h")
                            sp.dma_start(out[part * SP_:(part + 1) * SP_, :].rearrange("p (g h) -> p g h", h=SC), b).then_inc(sem["loaded"], 16)

                @block.tensor
                def _(pe):
                    pe.wait_ge(sem["loaded"], 16 * 13)
                    for i in range(2):
                        pe.transpose(bank[0][:, i * SG:(i + 1) * SG], rows[:, i, :], ident[0:SG, 0:SG])
                    pe.matmul(bank[0][:, 2 * SG:3 * SG], ones[0:1, :], dt_row[:, :], start=True, stop=True).then_inc(sem["turned"], 1)
                    for order in range(2):
                        for b in range(NB):
                            mm = pe.transpose(bank[1 + 2 * order + b // 4][:, (b % 4) * P:(b % 4 + 1) * P], c_rows[:, b, order, :], ident[:, :])
                    mm.then_inc(sem["turned"], 1)

                @block.scalar
                def _(act):
                    n = [0]

                    def do(out, in_, f, **k):
                        act.activation(t[out][:, :], t[in_][:, :], f, **k).then_inc(sem["act_step"], 1)
                        n[0] += 1
                        act.wait_ge(sem["act_step"], n[0])

                    act.wait_ge(sem["copied"], 1)
                    do("dt", "dt", ACT.Exp)
                    act.wait_ge(sem["copied"], 2)
                    do("mag", "mag_in", ACT.Exp)
                    act.wait_ge(sem["copied"], 3)
                    do("sn", "th", ACT.Sin)
                    do("cs", "x0", ACT.Sin)

                @block.vector
                def _(dve):
                    steps = Steps(dve, sem["step"])

                    def do(ins):
                        steps.did(ins)
                        steps.wait()

                    T_ = lambda n: t[n][:, :]
                    tt = lambda o, x, y, op: do(dve.tensor_tensor(T_(o), T_(x), T_(y), op))
                    ts = lambda o, x, c1, c2, o1, o2: do(dve.tensor_scalar(T_(o), T_(x), c1, c2, o1, o2))
                    do(dve.memset(sign[0:SP_, :], 1.0))
                    do(dve.memset(sign[SP_:P, :], -1.0))
                    dve.wait_ge(sem["turned"], 1)
                    do(dve.tensor_copy(T_("are"), bank[0][:, 0:SG]))
                    do(dve.tensor_copy(T_("aim"), bank[0][:, SG:2 * SG]))
                    do(dve.tensor_copy(T_("dt"), bank[0][:, 2 * SG:3 * SG]))
                    dve.sem_inc(sem["copied"], 1)
                    dve.wait_ge(sem["act_step"], 1)
                    tt("mag_in", "dt", "are", ALU.mult)
                    dve.sem_inc(sem["copied"], 1)
                    tt("th", "dt", "aim", ALU.mult)
                    ts("k", "th", 1.0 / (2 * math.pi), 12582912.0, ALU.mult, ALU.add)
                    ts("k", "k", 12582912.0, None, ALU.subtract, ALU.bypass)
                    c1 = 6.28125
                    c2 = float(np.float32(np.round((2 * math.pi - c1) * 2 ** 22) / 2 ** 22))
                    c3 = 2 * math.pi - c1 - c2
                    for c in (c1, c2, c3):
                        do(dve.scalar_tensor_tensor(out=T_("th"), in0=T_("k"), scalar=-c, in1=T_("th"), op0=ALU.mult, op1=ALU.add))
                    ts("th", "th", 3.1415925, -3.1415925, ALU.min, ALU.max)
                    ts("x1", "th", -1.0, None, ALU.mult, ALU.bypass)
                    tt("x0", "th", "x1", ALU.max)
                    ts("x0", "x0", -1.0, math.pi / 2, ALU.mult, ALU.add)
                    dve.sem_inc(sem["copied"], 1)
                    dve.wait_ge(sem["act_step"], 4)
                    tt("re", "mag", "cs", ALU.mult)
                    tt("im", "mag", "sn", ALU.mult)
                    ts("x0", "re", -1.0, None, ALU.add, ALU.bypass)
                    tt("cr", "x0", "are", ALU.mult)
                    tt("x1", "im", "aim", ALU.mult)
                    tt("cr", "cr", "x1", ALU.add)
                    tt("ci", "im", "are", ALU.mult)
                    tt("x1", "x0", "aim", ALU.mult)
                    tt("ci", "ci", "x1", ALU.subtract)
                    tt("den", "are", "are", ALU.mult)
                    tt("x1", "aim", "aim", ALU.mult)
                    tt("den", "den", "x1", ALU.add)
                    do(dve.reciprocal(T_("den"), T_("den")))
                    tt("cr", "cr", "den", ALU.mult)
                    tt("ci", "ci", "den", ALU.mult)
                    do(dve.tensor_scalar(T_("ci_s"), T_("ci"), sign[:, :], -1.0, ALU.mult, ALU.mult))
                    do(dve.memset(fwd[:, :, 0:1], 1.0))
                    do(dve.memset(fwd_s[:, :, 0:1], 0.0))
                    do(dve.memset(T_("cs"), 1.0))
                    do(dve.memset(T_("sn"), 0.0))
                    for n in range(1, CH + 1):
                        tt("x0", "cs", "re", ALU.mult)
                        tt("x1", "sn", "im", ALU.mult)
                        tt("mag", "cs", "im", ALU.mult)
                        tt("mag_in", "sn", "re", ALU.mult)
                        tt("cs", "x0", "x1", ALU.subtract)
                        tt("sn", "mag", "mag_in", ALU.add)
                        do(dve.tensor_copy(fwd[:, :, n], T_("cs")))
                        do(dve.tensor_scalar(fwd_s[:, :, n], T_("sn"), sign[:, :], -1.0, ALU.mult, ALU.mult))
                    for n in range(CH):
                        do(dve.tensor_copy(rev[:, :, n], fwd[:, :, CH - 1 - n]))
                        do(dve.tensor_copy(rev_s[:, :, n], fwd_s[:, :, CH - 1 - n]))
                    dve.wait_ge(sem["turned"], 2)
                    for order, out in ((0, Q1), (1, Q2)):
                        for half in range(2):
                            do(dve.tensor_scalar(out[:, half * T:(half + 1) * T], bank[1 + 2 * order + half][:, :], sign[:, :], None, ALU.mult))
                    wide = lambda n: t[n][:, :].unsqueeze(2).broadcast_to([P, SG, SC])
                    v = lambda x: x[:, :].rearrange("p (g h) -> p g h", h=SC)
                    with Scope(nc, "ssm_b") as s3:
                        p1, p2 = s3.sb("p1", [P, SG * SC]), s3.sb("p2", [P, SG * SC])
                        do(dve.tensor_tensor(v(p1), v(B2), wide("ci_s"), ALU.mult))
                        do(dve.tensor_tensor(v(p2), v(B1), wide("ci_s"), ALU.mult))
                        do(dve.tensor_tensor(v(B1), v(B1), wide("cr"), ALU.mult))
                        do(dve.tensor_tensor(v(B2), v(B2), wide("cr"), ALU.mult))
                        do(dve.tensor_tensor(v(B1), v(B1), v(p1), ALU.add))
                        do(dve.tensor_tensor(v(B2), v(B2), v(p2), ALU.subtract))

        u = s.sb("u", [NCH, CH, SG * SC])
        skip = s.sb("skip", [NCH, SG * SC])
        CA = s.sb("CA", [P, NB, GB, CH + 1, SC])
        states = s.sb("states", [P, NCH + 1, 2, SG])
        with Scope(nc, "ssm_chunks") as s2:
            names = ["loaded", "zeroed", "zeroed2", "sliced", "ba", "shifts", "ca", "u_turned", "u_ready", "ba_turned", "ba_ready",
                     "b_mm", "b_ready", "m_mm", "m_ready", "y_mm", "y_ready", "dve_step", "skipped", "passed", "passed_dve", "y_first"]
            sem = {n: s2.sem(n) for n in names}
            u_b = s2.sb("u_b", [NCH, GB, CH, SC])
            BA, part = s2.sb("BA", [P, GB, CH, SC]), s2.sb("part", [P, GB, CH + 1, SC])
            shift = s2.sb("shift", [P, GB, 15, SC])
            U = s2.sb("U", [P, GB, NCH])
            IT = s2.sb("IT", [P, GB, 3 * SP_])
            M = s2.sb("M", [P, GB, P])
            du = s2.sb("du", [NCH, CH, P])
            bank = s2.banks()
            with nc.Block() as block:
                @block.sync
                def _(sp):
                    sp.dma_start(u[:, :, :], u_dram.rearrange("(c t) n -> c t n", t=CH)).then_inc(sem["loaded"], 16)
                    sp.dma_start(skip[:, :], a["D_skip_2"].rearrange("g h -> (g h)").unsqueeze(0).broadcast_to([NCH, SG * SC])).then_inc(sem["loaded"], 16)

                @block.gpsimd
                def _(pool):
                    pool.memset(shift[:, :, :, :], 0.0).then_inc(sem["zeroed"], 1)
                    pool.sem_inc(sem["u_turned"], 1)
                    pool.wait_ge(sem["loaded"], 32)
                    with pool.Fori(0, NB) as b:
                        pool.wait_ge(sem["u_turned"], b + 1)
                        cut = bass.ds(b * P, P)
                        pool.tensor_copy(u_b[:, :, :, :].rearrange("c g t n -> c t g n"),
                                         u[:, :, cut].rearrange("c t (g n) -> c t g n", n=SC)).then_inc(sem["sliced"], 1)
                        pool.wait_ge(sem["y_ready"], b + 1)
                        pool.tensor_tensor(du[:, :, :], u[:, :, cut], skip[:, cut].unsqueeze(1).broadcast_to([NCH, CH, P]),
                                           ALU.mult).then_inc(sem["skipped"], 1)

                @block.vector
                def _(dve):
                    dve.sem_inc(sem["y_ready"], 1)
                    dve.memset(states[:, 0, :, :], 0.0).then_inc(sem["zeroed2"], 1)
                    dve.wait_ge(sem["zeroed2"], 1)
                    dve.wait_ge(sem["zeroed"], 1)

                    def chan(x, b):
                        return x[:, bass.ds(b * P, P)].rearrange("p (g h) -> p g h", h=SC)

                    def build(b, first=False):
                        g = bass.ds(b * GB, GB)
                        if not first:
                            dve.wait_ge(sem["ba_turned"], b)
                            dve.wait_ge(sem["ca"], b)
                        for out, x, w in ((BA, B1, rev), (part, B2, rev_s)):
                            dve.tensor_tensor(out[:, :, 0:CH, :], chan(x, b).unsqueeze(2).broadcast_to([P, GB, CH, SC]),
                                              w[:, g, :].unsqueeze(3).broadcast_to([P, GB, CH, SC]), ALU.mult).then_inc(sem["dve_step"], 1)
                        dve.wait_ge(sem["dve_step"], 4 * b + 2)
                        dve.tensor_tensor(BA[:, :, :, :], BA[:, :, :, :], part[:, :, 0:CH, :], ALU.add).then_inc(sem["ba"], 1)
                        if not first:
                            dve.wait_ge(sem["m_mm"], b)
                            dve.sem_inc(sem["passed_dve"], 1)
                        dve.tensor_copy(shift[:, :, 7, :], chan(B1, b)).then_inc(sem["shifts"], 1)
                        dve.wait_ge(sem["ba"], b + 1)
                        now = CA[:, bass.ds(b, 1), :, :, :].rearrange("p o g n h -> p (o g) n h")
                        for out, x, w in ((now, Q1, fwd), (part[:, :, :, :], Q2, fwd_s)):
                            dve.tensor_tensor(out, chan(x, b).unsqueeze(2).broadcast_to([P, GB, CH + 1, SC]),
                                              w[:, g, :].unsqueeze(3).broadcast_to([P, GB, CH + 1, SC]), ALU.mult).then_inc(sem["dve_step"], 1)
                        dve.wait_ge(sem["dve_step"], 4 * b + 4)
                        dve.tensor_tensor(now, now, part[:, :, :, :], ALU.add).then_inc(sem["ca"], 1)

                    def collect(b):
                        for h in range(2):
                            dve.wait_ge(sem["b_mm"], 2 * b + h + 1)
                            src = bank[5 + h][:, :].rearrange("p (g v c) -> p c v g", v=2, c=NCH)
                            for v in range(2):
                                dve.tensor_copy(states[:, 1:NCH + 1, v, bass.ds(b * GB + 4 * h, 4)], src[:, :, v, :]).then_inc(sem["b_ready"], 1)
                        dve.wait_ge(sem["skipped"], b + 1)
                        dve.wait_ge(sem["y_mm"], b + 1)
                        for h in range(2):
                            src = bank[(7, 1)[h]][0:NCH, :].rearrange("c (g t n) -> c t g n", g=4, n=SC)
                            add = du[:, :, h * 64:(h + 1) * 64].rearrange("c t (g n) -> c t g n", n=SC)
                            out = u[:, :, bass.ds(b * P + h * 64, 64)].rearrange("c t (g n) -> c t g n", n=SC)
                            if h == 1:
                                dve.wait_ge(sem["y_first"], b + 1)
                            dve.tensor_tensor(out, src, add, ALU.add).then_inc(sem["y_first"] if h == 0 else sem["y_ready"], 1)

                    build(0, first=True)
                    with dve.Fori(0, NB - 1) as b:
                        build(b + 1)
                        collect(b)
                    collect(NB - 1)
                    dve.wait_ge(sem["y_ready"], NB + 1)

                @block.tensor
                def _(pe):
                    with pe.Fori(0, NB) as b:
                        pe.wait_ge(sem["sliced"], b + 1)
                        pe.sem_inc(sem["passed"], 1)
                        for g in range(GB):
                            mm = pe.transpose(bank[0][:, g * NCH:(g + 1) * NCH], u_b[:, g, :, :], ident[0:NCH, 0:NCH])
                        mm.then_inc(sem["u_turned"], 1)
                        pe.wait_ge(sem["shifts"], b + 1)
                        pe.wait_ge(sem["ca"], b + 1)
                        for g in range(GB):
                            for st in range(CH):
                                mm = pe.matmul(bank[3 + g // 4][:, (g % 4) * P + st * SC:(g % 4 + 1) * P],
                                               shift[:, g, 7 - st:15 - st, :],
                                               CA[:, bass.ds(b, 1), g, 0:CH - st, :], start=(st == 0), stop=(st == CH - 1),
                                               skip_group_check=True)
                        mm.then_inc(sem["m_mm"], 1)
                        pe.wait_ge(sem["y_ready"], b + 1)
                        pe.sem_inc(sem["passed"], 1)
                        for g in range(GB):
                            mm = pe.transpose(bank[1 + g // 4][:, (g % 4) * P:(g % 4 + 1) * P], BA[:, g, :, :], ident[:, :])
                        mm.then_inc(sem["ba_turned"], 1)
                        pe.wait_ge(sem["u_ready"], b + 1)
                        pe.wait_ge(sem["ba_ready"], 4 * b + 4)
                        for g in range(GB):
                            for v in range(2):
                                mm = pe.matmul(bank[5 + g // 4][:, (g % 4) * P + v * NCH:(g % 4) * P + (v + 1) * NCH],
                                               IT[:, g, v * SP_:v * SP_ + P], U[:, g, :], start=True, stop=True)
                            if g % 4 == 3:
                                mm.then_inc(sem["b_mm"], 1)
                        pe.wait_ge(sem["m_ready"], 2 * b + 2)
                        for g in range(GB):
                            mm = pe.matmul(bank[(7, 1)[g // 4]][0:NCH, (g % 4) * P:(g % 4 + 1) * P], U[:, g, :], M[:, g, :],
                                           start=True, stop=True)
                        mm.then_inc(sem["y_mm"], 1)

                @block.scalar
                def _(act):
                    with act.Fori(0, NB) as b:
                        act.wait_ge(sem["u_turned"], b + 2)
                        act.activation(U[:, :, :], bank[0][:, :].rearrange("p (g c) -> p g c", c=NCH), ACT.Copy).then_inc(sem["u_ready"], 1)
                        act.wait_ge(sem["m_mm"], b + 1)
                        for h in range(2):
                            act.activation(M[:, 4 * h:4 * h + 4, :], bank[3 + h][:, :].rearrange("p (g n) -> p g n", n=P),
                                           ACT.Copy).then_inc(sem["m_ready"], 1)
                        act.wait_ge(sem["ba_turned"], b + 1)
                        for h in range(2):
                            src = bank[1 + h][:, :].rearrange("p (g n) -> p g n", n=P)
                            act.activation(IT[:, 4 * h:4 * h + 4, 0:P], src, ACT.Copy).then_inc(sem["ba_ready"], 1)
                            act.activation(IT[:, 4 * h:4 * h + 4, P:3 * SP_], src[:, :, 0:SP_], ACT.Copy).then_inc(sem["ba_ready"], 1)

        with Scope(nc, "ssm_scan") as s2:
            a_re, a_im = s2.sb("a_re", [P, 2, SG]), s2.sb("a_im", [P, 2, SG])
            p1, p2, p3 = (s2.sb(n, [P, 2, SG]) for n in ("p1", "p2", "p3"))
            now = s2.sb("now", [P, 2, NCH, GB])
            names = ["set", "p1", "p2", "p3", "state", "sliced", "y_mm", "y_sum", "gelu", "turned", "out"]
            sem = {n: s2.sem(n) for n in names}
            bank = s2.banks()
            with nc.Block() as block:
                @block.vector
                def _(dve):
                    for v in range(2):
                        dve.tensor_copy(a_re[:, v, :], fwd[:, :, CH]).then_inc(sem["set"], 1)
                    dve.tensor_copy(a_im[:, 0, :], fwd_s[:, :, CH]).then_inc(sem["set"], 1)
                    dve.tensor_scalar(a_im[:, 1, :], fwd_s[:, :, CH], -1.0, None, ALU.mult).then_inc(sem["set"], 1)
                    dve.wait_ge(sem["set"], 4)
                    dve.sem_inc(sem["state"], 1)
                    with dve.Fori(0, NCH - 1) as c:
                        dve.wait_ge(sem["state"], c + 1)
                        old = states[:, bass.ds(c, 1), :, :].rearrange("p o v g -> p (o v) g")
                        new = states[:, bass.ds(c + 1, 1), :, :].rearrange("p o v g -> p (o v) g")
                        dve.tensor_tensor(p1[:, :, :], old, a_re[:, :, :], ALU.mult).then_inc(sem["p1"], 1)
                        for v in range(2):
                            dve.tensor_tensor(p2[:, v, :], states[:, bass.ds(c, 1), 1 - v, :], a_im[:, v:v + 1, :], ALU.mult).then_inc(sem["p2"], 1)
                        dve.wait_ge(sem["p1"], c + 1)
                        dve.tensor_tensor(p3[:, :, :], p1[:, :, :], new, ALU.add).then_inc(sem["p3"], 1)
                        dve.wait_ge(sem["p2"], 2 * c + 2)
                        dve.wait_ge(sem["p3"], c + 1)
                        dve.tensor_tensor(new, p3[:, :, :], p2[:, :, :], ALU.add).then_inc(sem["state"], 1)
                    dve.sem_inc(sem["y_sum"], 4)
                    with dve.Fori(0, NB // 2) as i:
                        for two in range(2):
                            b = 2 * i + two
                            dve.wait_ge(sem["y_mm"], b + 1)
                            for h in range(2):
                                src = bank[2 * two + h][0:NCH, :].rearrange("c (g t n) -> c t g n", g=4, n=SC)
                                at = u[:, :, bass.ds(b * P + h * 64, 64)].rearrange("c t (g n) -> c t g n", n=SC)
                                dve.tensor_tensor(at, src, at, ALU.add).then_inc(sem["y_sum"], 1)

                @block.gpsimd
                def _(pool):
                    pool.wait_ge(sem["state"], NCH)
                    with pool.Fori(0, NB // 2) as i:
                        for two in range(2):
                            b = 2 * i + two
                            pool.wait_ge(sem["y_sum"], 2 * b + 2)
                            pool.tensor_copy(now[:, two, :, :], states[:, 0:NCH, 0, bass.ds(b * GB, GB)]).then_inc(sem["sliced"], 1)

                @block.tensor
                def _(pe):
                    with pe.Fori(0, NB // 2) as i:
                        for two in range(2):
                            b = 2 * i + two
                            pe.wait_ge(sem["sliced"], b + 1)
                            for g in range(GB):
                                mm = pe.matmul(bank[2 * two + g // 4][0:NCH, (g % 4) * P:(g % 4 + 1) * P], now[:, two, :, g],
                                               CA[:, bass.ds(b, 1), g, 1:CH + 1, :], start=True, stop=True)
                            mm.then_inc(sem["y_mm"], 1)
                    for t_ in range(CH):
                        pe.wait_ge(sem["gelu"], t_ + 1)
                        if t_ == 0:
                            pe.wait_ge(sem["y_sum"], 2 * NB + 4)
                    for tile in range(8):
                        if tile >= 4:
                            pe.wait_ge(sem["out"], tile - 3)
                        for t_ in range(CH):
                            mm = pe.transpose(bank[4 + tile % 4][:, t_ * NCH:(t_ + 1) * NCH], u[:, t_, tile * P:(tile + 1) * P],
                                              ident[0:NCH, 0:NCH])
                        mm.then_inc(sem["turned"], 1)

                @block.scalar
                def _(act):
                    act.wait_ge(sem["y_sum"], 2 * NB + 4)
                    for t_ in range(CH):
                        act.activation(u[:, t_, :], u[:, t_, :], ACT.Gelu_apprx_tanh).then_inc(sem["gelu"], 1)
                    for tile in range(8):
                        act.wait_ge(sem["turned"], tile + 1)
                        act.activation(y_T[:, tile, :].rearrange("p (c t) -> p t c", t=CH),
                                       bank[4 + tile % 4][:, :].rearrange("p (t c) -> p t c", c=NCH), ACT.Copy).then_inc(sem["out"], 1)
                    act.wait_ge(sem["out"], 8)


def block_one_mix(nc, a, cols, ident, ones, block_ones, mixed_T):
    with Scope(nc, "mix") as s:
        rwkv_T = s.sb("rwkv_T", [P, RT, 1 + T])
        with Scope(nc, "mix_in") as s2:
            u_T = s2.sb("u_T", [P, KD, T])
            taps = s2.sb("taps", [P, CT, CW])
            load_taps(nc, a["conv_dw"][0], ident, taps)
            with Scope(nc, "first_norm") as s3:
                rows = s3.sb("rows", [P, TT, D])
                load_rows(nc, "x_in", a["x"][0], rows)
                norm_transpose(nc, "norm_mix", rows, cols["norm_mix"], ident, u_T, 1e-6)
            ring = [s2.sb(f"ring{i}", [P, KD, T]) for i in range(2)]
            project_in(nc, a["w_in"][0], u_T, ring, mixed_T, rwkv_T, taps, cols["conv_b"], cols["shift_mu"])
        conv_norm(nc, mixed_T, ones, cols["conv_ln_g"], cols["conv_ln_b"])
        rwkv(nc, a, cols, ident, block_ones, rwkv_T, mixed_T)


def token_panels(nc, name, ring, left_T, KT, pairs, weights, stage, out, left_copy):
    with Scope(nc, name) as s:
        g = Gemm(nc, s, ring, left_T, KT, pairs, weights, False)
        stored, kept = s.sem("stored"), s.sem("kept")
        with nc.Block() as block:
            @block.sync
            def _(sp):
                g.sync(sp)
                sp.dma_start(left_copy, left_T[:, :, :]).then_inc(kept, 16)
                sp.wait_ge(kept, 16)
                sp.wait_ge(g.bank_free, BANKS * (pairs + 1))
                sp.dma_start(out.rearrange("(t p) d -> p t d", p=P), stage[:, :, :]).then_inc(stored, 16)
                sp.wait_ge(stored, 16)

            block.tensor(g.tensor)

            @block.scalar
            def _(act):
                def copy(bank, panel, sub, b, i):
                    act.activation(stage[:, sub, bass.ds(panel * T, T)], bank[:, :], ACT.Copy).then_inc(g.bank_free, 1)

                g.drain(act, 0, pairs, copy)


def move(nc, name, pairs):
    with Scope(nc, name) as s:
        moved = s.sem("moved")
        with nc.Block() as block:
            @block.sync
            def _(sp):
                for out, in_ in pairs:
                    sp.dma_start(out, in_).then_inc(moved, 16)
                sp.wait_ge(moved, 16 * len(pairs))


def block_one(nc, a, cols, gain, ident, ones, block_ones, gates):
    hidden = nc.dram_tensor("hidden", (T, D), F32, kind="Internal").ap()
    normed = nc.dram_tensor("normed", (T, D), F32, kind="Internal").ap()
    results = nc.dram_tensor("results", (2 * T, D), F32, kind="Internal").ap()
    id_table = nc.dram_tensor("id_table", (SLOTS, 1), I32, kind="Internal").ap()
    with Scope(nc, "one") as s:
        table, takes = s.sb("table", [P, E + OVER], I32), s.sb("takes", [P, E + OVER], I32)
        over_expert, over_count = s.sb("over_expert", [1, OVER], I32), s.sb("over_count", [1, 1], I32)
        with Scope(nc, "one_mix") as s2:
            mixed_T = s2.sb("mixed_T", [P, KD, T])
            block_one_mix(nc, a, cols, ident, ones, block_ones, mixed_T)
            clear_semaphores(nc)
            rows = s2.sb("rows", [P, TT, D])
            with Scope(nc, "one_out") as s3:
                ring = [s3.sb(f"ring{i}", [P, KD, T]) for i in range(2)]
                project_out(nc, a["w_out"][0], mixed_T, rows, KD, 2, a["x"][0], ring, "project_one", out=hidden)
            v_T = s2.sb("v_T", [P, KD, T])
            norm_transpose(nc, "norm_ffn", rows, gain, ident, v_T, 1e-6)
            route(nc, a, v_T, ones, gates, table, over_expert, over_count, id_table, rows, normed)
        with Scope(nc, "takes") as s2, nc.Block() as block:
            halved = s2.sem("halved")

            @block.vector
            def _(dve):
                dve.tensor_scalar(takes[:, :], table[:, :], 1, None, ALU.logical_shift_right).then_inc(halved, 1)
                dve.wait_ge(halved, 1)
        clear_semaphores(nc)
        experts(nc, a, gain, ident, normed, results, table, takes)
        overflow(nc, a, gain, ident, normed, results, table, takes, over_expert, over_count)
    return hidden, results


def block_two(nc, a, cols, ident, ones, block_ones, hidden, results, gates, x2, out):
    u_dram = nc.dram_tensor("u_rows", (T, D // 2), F32, kind="Internal").ap()
    w_in = a["w_in_2"]

    def panels(w, first):
        return lambda panel: w[:, bass.ds((panel + first) * T, T)]

    def tile(panel, sub):
        return bass.ds(4 * panel + sub, 1)

    def flat(x, panel, sub):
        return x[:, tile(panel, sub), :].rearrange("p o t -> p (o t)")

    def copy_to(left):
        return lambda act, bank, panel, sub: act.activation(flat(left, panel, sub), bank[:, :], ACT.Copy)

    with Scope(nc, "two") as s:
        y_T = s.sb("y_T", [P, 8, T])
        h_dram = nc.dram_tensor("h_T", (P, KD * T), F32, kind="Internal").ap().rearrange("p (k t) -> p k t", t=T)
        with Scope(nc, "two_start") as s2:
            h_T = s2.sb("h_T", [P, KD, T])
            with Scope(nc, "two_norm") as s3:
                rows = s3.sb("rows", [P, TT, D])
                finish_block_one(nc, results, gates, hidden, a["norm_final"], rows, x2)
                norm_transpose(nc, "norm_two", rows, cols["norm_w_2"], ident, h_T, 1e-6)
            ring = [s2.sb(f"ring{i}", [P, KD, T]) for i in range(2)]
            stage = s2.sb("stage", [P, TT, D // 2])
            token_panels(nc, "project_u", ring, h_T, KD, 1, panels(w_in, 5), stage, u_dram, h_dram)
        clear_semaphores(nc)
        ssm(nc, a, u_dram, y_T, ident, ones)
        clear_semaphores(nc)
        merged_T = s.sb("merged_T", [P, KD, T])
        with Scope(nc, "two_attention") as s2:
            att_T = s2.sb("att_T", [P, 20, T])
            with Scope(nc, "two_attention_in") as s3:
                ring = [s3.sb(f"ring{i}", [P, KD, T]) for i in range(2)]
                h_T = s3.sb("h_T", [P, KD, T])
                move(nc, "h_in", [(h_T[:, :, :], h_dram)])
                linear(nc, "project_attention", ring, h_T, KD, 2, panels(w_in, 0), copy_to(att_T), odd=True)
            attention(nc, att_T, ident, block_ones, cols["q_norm_w_2"], cols["k_norm_w_2"], a["sinks_2"], ones)
            ring = [s2.sb(f"ring{i}", [P, 8, T]) for i in range(2)]
            linear(nc, "attention_out", ring, att_T, 8, 2, panels(a["w_attn_proj_2"], 0), copy_to(merged_T))
        ring = [s.sb(f"ring{i}", [P, KD, T]) for i in range(2)]
        half = [r[:, 0:8, :] for r in ring]
        h_T = s.sb("h_T", [P, KD, T])
        move(nc, "h_back", [(h_T[:, :, :], h_dram)])

        clear_semaphores(nc)

        def sigmoid(act, stage, bank, panel, sub):
            return act.activation(stage, bank[:, :], ACT.Sigmoid)

        def times(left):
            def combine(dve, stage, panel, sub):
                at = flat(left, panel, sub)
                return [lambda: dve.tensor_tensor(at, at, stage, ALU.mult)]
            return combine

        gated(nc, "gate_a", ring, h_T, KD, 2, panels(w_in, 9), sigmoid, times(merged_T))
        with Scope(nc, "two_glu") as s2:
            value_T = s2.sb("value_T", [P, 8, T])
            b_glu = cols["b_glu_2"]
            linear(nc, "glu_value", half, y_T, 8, 1, panels(a["w_glu_2"], 0),
                   lambda act, bank, panel, sub: act.activation(flat(value_T, panel, sub), bank[:, :], ACT.Identity,
                                                                bias=b_glu[:, bass.ds(4 * panel + sub, 1)]))
            gated(nc, "glu_gate", half, y_T, 8, 1, panels(a["w_glu_2"], 2),
                  lambda act, stage, bank, panel, sub: act.activation(stage, bank[:, :], ACT.Sigmoid,
                                                                      bias=b_glu[:, bass.ds(8 + 4 * panel + sub, 1)]),
                  times(value_T))
            gated(nc, "glu_z", ring, h_T, KD, 1, panels(w_in, 7),
                  lambda act, stage, bank, panel, sub: act.activation(stage, bank[:, :], ACT.Silu),
                  lambda dve, stage, panel, sub: [lambda: dve.tensor_tensor(flat(y_T, panel, sub), flat(value_T, panel, sub), stage, ALU.mult)])
        with Scope(nc, "two_ssm_out") as s2:
            part_T = s2.sb("part_T", [P, KD, T])
            linear(nc, "ssm_out", half, y_T, 8, 2, panels(a["w_ssm_proj_2"], 0), copy_to(part_T))

            def add(dve, stage, panel, sub):
                at, part = flat(merged_T, panel, sub), flat(part_T, panel, sub)
                return [lambda: dve.tensor_tensor(part, part, stage, ALU.mult),
                        lambda: dve.tensor_tensor(at, at, part, ALU.add)]

            gated(nc, "gate_s", ring, h_T, KD, 2, panels(w_in, 13), sigmoid, add)
        rows = s.sb("rows", [P, TT, D])
        project_out(nc, a["w_out_2"], merged_T, rows, KD, 2, x2, ring, "project_two", out=out)


def two_blocks(nc, a, out):
    x2 = nc.dram_tensor("x2", (T, D), F32, kind="Internal").ap()
    Scope.spent = []
    with Scope(nc, "whole") as s:
        ident, ones, block_ones = (s.sb(n, [P, P]) for n in ("ident", "ones", "block_ones"))
        constants(nc, ident, ones, block_ones)
        layered = ["norm_mix", "conv_b", "conv_ln_g", "conv_ln_b", "shift_mu", "w0", "a0", "k_k", "k_a", "gn_g", "gn_b"]
        cols = Columns(nc, s, "one", [(n, a[n][0]) for n in layered] + [("r_k", a["r_k"][0].rearrange("h d -> (h d)"))])
        more = Columns(nc, s, "two", [("norm_ffn", a["norm_ffn"][0])] + [(n, a[n]) for n in ("norm_w_2", "b_glu_2")],
                       twice=[("q_norm_w_2", a["q_norm_w_2"]), ("k_norm_w_2", a["k_norm_w_2"])])
        load_columns(nc, ident, cols.rows, cols.tile)
        load_columns(nc, ident, more.rows, more.tile)
        gates = s.sb("gates", [P, TT, 2])
        hidden, results = block_one(nc, a, cols, more["norm_ffn"], ident, ones, block_ones, gates)
        clear_semaphores(nc)
        block_two(nc, a, more, ident, ones, block_ones, hidden, results, gates, x2, out)


_INS = ["x", "norm_mix", "w_in", "conv_dw", "conv_b", "conv_ln_g", "conv_ln_b", "shift_mu", "w0", "w_lora_up", "a0",
        "a_lora_up", "g_lora_up", "k_k", "k_a", "r_k", "gn_g", "gn_b", "w_out", "norm_ffn", "router_group_w",
        "router_group_b", "router_expert_w", "router_expert_b", "expert_w_gate", "expert_w_up", "expert_w_down",
        "norm_final", "norm_w_2", "w_in_2", "q_norm_w_2", "k_norm_w_2", "sinks_2", "w_attn_proj_2", "A_re_2", "A_im_2",
        "log_dt_2", "B_re_2", "B_im_2", "C_re_2", "C_im_2", "D_skip_2", "w_glu_2", "b_glu_2", "w_ssm_proj_2", "w_out_2"]
_OUTS = [((1, T, D), "float32")]


def kernel(**inputs):
    import numpy as _np
    import concourse.bacc as _bacc
    from concourse import mybir as _mybir
    from concourse.bass_utils import run_bass_kernel_spmd as _run

    nc = _bacc.Bacc("TRN2", target_bir_lowering=False, num_devices=1)
    arrays, args = {}, {}
    for name in _INS:
        a = _np.ascontiguousarray(inputs[name])
        arrays[f"in_{name}"] = a
        args[name] = nc.dram_tensor(f"in_{name}", a.shape, _mybir.dt.from_np(a.dtype), kind="ExternalInput").ap()
    out = nc.dram_tensor("out_0", _OUTS[0][0], _mybir.dt.from_np(_np.dtype(_OUTS[0][1])), kind="ExternalOutput").ap()
    two_blocks(nc, args, out[0])
    r = _run(nc, [arrays], core_ids=[0])
    return r.results[0]["out_0"]
```
